# Optimizing a Trainium2 kernel written in Bass

```python
import math
import jax, jax.numpy as jnp
from jax import lax
import numpy as np

D_MODEL = 1024
BATCH = 1
SEQ = 1024
DEPTH = 1
DEC_BATCH = 8
DEC_SEQ = 8
PAST_LEN = 256
PAGE_SIZE = 128

D_MIX = D_MODEL
HEAD_DIM = 64
D_SB = D_MIX // 2
D_DIL = D_MIX - D_SB
N_HEADS_SB = D_SB // HEAD_DIM
N_HEADS_DIL = D_DIL // HEAD_DIM
DILATIONS = ((128, 1), (512, 4), (2048, 16))
MAX_WINDOW = 2048
Q_BLOCK = 128
NORM_EPS = 1e-6
SB_BIAS_INIT = -7.0
F32 = jnp.float32

kernel_name = 'hymba_stickbreak_dilated_alibi_step'

def alibi_slopes(n_heads):
    return jnp.exp2(-8.0 * jnp.arange(1, n_heads + 1, dtype=F32) / n_heads)

def rmsnorm(x, w):
    xf = x.astype(F32)
    y = xf * lax.rsqrt(jnp.mean(xf * xf, axis=-1, keepdims=True) + NORM_EPS)
    return (y * w.astype(F32)).astype(x.dtype)

def in_projection(h, w_in):
    proj = jnp.einsum('btd,de->bte', h, w_in)
    b, t, _ = proj.shape
    bounds = [D_SB, 2 * D_SB, 3 * D_SB, 4 * D_SB,
              4 * D_SB + D_DIL, 4 * D_SB + 2 * D_DIL, 4 * D_SB + 3 * D_DIL]
    q_sb, k_sb, v_sb, g_sb, q_dl, k_dl, v_dl, g_dl = jnp.split(proj, bounds, axis=-1)
    hs = lambda a, n: a.reshape(b, t, n, HEAD_DIM)
    return (hs(q_sb, N_HEADS_SB), hs(k_sb, N_HEADS_SB), hs(v_sb, N_HEADS_SB), g_sb,
            hs(q_dl, N_HEADS_DIL), hs(k_dl, N_HEADS_DIL), hs(v_dl, N_HEADS_DIL), g_dl)

def stick_breaking(q, k, v, q_pos, bias):
    z = jnp.einsum('bqhd,bshd->bhqs', q, k, preferred_element_type=F32) * (HEAD_DIM ** -0.5)
    z = z + bias.astype(F32)[None, :, None, None]
    s_pos = jnp.arange(k.shape[1])
    mask = s_pos[None, :] < q_pos[:, None]
    log_keep = jnp.where(mask, jax.nn.log_sigmoid(-z), 0.0)
    later = jnp.concatenate([log_keep[..., 1:], jnp.zeros_like(log_keep[..., :1])], axis=-1)
    log_remain = lax.cumsum(later, axis=3, reverse=True)
    a = jnp.where(mask, jnp.exp(jax.nn.log_sigmoid(z) + log_remain), 0.0)
    return jnp.einsum('bhqs,bshd->bqhd', a.astype(v.dtype), v, preferred_element_type=F32)

def stick_breaking_prompt(q, k, v, bias):
    b, t, h, dh = q.shape
    n_blk = t // Q_BLOCK

    def one_block(i):
        qb = lax.dynamic_slice_in_dim(q, i * Q_BLOCK, Q_BLOCK, axis=1)
        return stick_breaking(qb, k, v, i * Q_BLOCK + jnp.arange(Q_BLOCK), bias)

    out = lax.map(one_block, jnp.arange(n_blk))
    return out.transpose(1, 0, 2, 3, 4).reshape(b, t, h, dh)

def dilated_prompt(q, k, v, slopes, window, dilation):
    b, t, h, dh = q.shape
    n_steps = window // dilation
    span = dilation * Q_BLOCK
    t_pad = -(-t // span) * span
    pad = ((0, 0), (0, t_pad - t), (0, 0), (0, 0))

    def to_blocks(a):
        a = jnp.pad(a, pad).reshape(b, t_pad // dilation, dilation, h, dh).transpose(0, 2, 1, 3, 4)
        return a.reshape(b, dilation, -1, Q_BLOCK, h, dh)

    def with_prev(a):
        prev = jnp.pad(a[:, :, :-1], ((0, 0), (0, 0), (1, 0), (0, 0), (0, 0), (0, 0)))
        return jnp.concatenate([prev, a], axis=3)

    qb = to_blocks(q)
    kk, vv = with_prev(to_blocks(k)), with_prev(to_blocks(v))
    n_blk = qb.shape[2]
    steps = Q_BLOCK + jnp.arange(Q_BLOCK)[:, None] - jnp.arange(2 * Q_BLOCK)[None, :]
    blk_ok = (jnp.arange(n_blk)[:, None, None] > 0) | (jnp.arange(2 * Q_BLOCK)[None, None, :] >= Q_BLOCK)
    valid = (steps >= 0) & (steps <= n_steps) & blk_ok
    s = jnp.einsum('brnqhd,brnkhd->brnhqk', qb, kk, preferred_element_type=F32) * (HEAD_DIM ** -0.5)
    s = s - slopes[:, None, None] * (steps * dilation).astype(F32)
    s = jnp.where(valid[:, None], s, -jnp.inf)
    lse = jax.nn.logsumexp(s, axis=-1)
    p = jnp.exp(s - lse[..., None])
    o = jnp.einsum('brnhqk,brnkhd->brnqhd', p.astype(vv.dtype), vv, preferred_element_type=F32)

    def from_blocks(a):
        a = a.reshape(b, dilation, t_pad // dilation, *a.shape[4:])
        a = jnp.moveaxis(a, 1, 2).reshape(b, t_pad, *a.shape[3:])
        return a[:, :t]

    return from_blocks(o), from_blocks(lse.transpose(0, 1, 2, 4, 3))

def dilated_sample(q, k_ext, v_ext, slopes, window, dilation):
    s_new = q.shape[1]
    n_prev = k_ext.shape[1] - s_new
    steps = jnp.arange(window // dilation + 1)
    idx = n_prev + jnp.arange(s_new)[:, None] - steps[None, :] * dilation
    valid = idx >= 0
    idx = jnp.maximum(idx, 0)
    kg = k_ext[:, idx]
    vg = v_ext[:, idx]
    s = jnp.einsum('bqhd,bqjhd->bhqj', q, kg, preferred_element_type=F32) * (HEAD_DIM ** -0.5)
    s = s - slopes[:, None, None] * (steps * dilation).astype(F32)[None, None, :]
    s = jnp.where(valid, s, -jnp.inf)
    lse = jax.nn.logsumexp(s, axis=-1)
    p = jnp.exp(s - lse[..., None])
    o = jnp.einsum('bhqj,bqjhd->bqhd', p.astype(vg.dtype), vg, preferred_element_type=F32)
    return o, lse.transpose(0, 2, 1)

def combine_by_denominator(outs, lses):
    w = jax.nn.softmax(jnp.stack(lses, 0), axis=0)
    return jnp.sum(w[..., None] * jnp.stack(outs, 0), axis=0)

def gated_branch(o, g, norm_w):
    b, t, h, dh = o.shape
    y = o * lax.rsqrt(jnp.mean(o * o, axis=-1, keepdims=True) + NORM_EPS)
    y = y.reshape(b, t, h * dh) * norm_w.astype(F32)
    return y * jax.nn.silu(g.astype(F32))

def mix_out(o_sb, g_sb, o_dl, g_dl, sb_norm_w, dil_norm_w, w_out):
    y = jnp.concatenate([gated_branch(o_sb, g_sb, sb_norm_w),
                         gated_branch(o_dl, g_dl, dil_norm_w)], axis=-1).astype(w_out.dtype)
    return jnp.einsum('bte,ed->btd', y, w_out)

def prompt_layer(x, slopes, pre_w, w_in, sb_b, sb_w, dl_w, w_out, post_w):
    h = rmsnorm(x, pre_w)
    q_sb, k_sb, v_sb, g_sb, q_dl, k_dl, v_dl, g_dl = in_projection(h, w_in)
    o_sb = stick_breaking_prompt(q_sb, k_sb, v_sb, sb_b)
    res = [dilated_prompt(q_dl, k_dl, v_dl, slopes, w, r) for (w, r) in DILATIONS]
    o_dl = combine_by_denominator([a for a, _ in res], [c for _, c in res])
    m = mix_out(o_sb, g_sb, o_dl, g_dl, sb_w, dl_w, w_out)
    y = x + rmsnorm(m, post_w).astype(x.dtype)
    keep = min(MAX_WINDOW, x.shape[1])
    return y, k_sb, v_sb, k_dl[:, -keep:], v_dl[:, -keep:]

def sample_layer(x, k_pool, v_pool, k_win, v_win, page_table, slopes,
                 pre_w, w_in, sb_b, sb_w, dl_w, w_out, post_w):
    db, s_new, _ = x.shape
    h = rmsnorm(x, pre_w)
    q_sb, k_sb, v_sb, g_sb, q_dl, k_dl, v_dl, g_dl = in_projection(h, w_in)
    n_pages, page = page_table.shape[1], k_pool.shape[1]
    past = n_pages * page
    k_past = k_pool[page_table].reshape(db, past, N_HEADS_SB, HEAD_DIM)
    v_past = v_pool[page_table].reshape(db, past, N_HEADS_SB, HEAD_DIM)
    k_all = jnp.concatenate([k_past, k_sb.astype(k_past.dtype)], axis=1)
    v_all = jnp.concatenate([v_past, v_sb.astype(v_past.dtype)], axis=1)
    o_sb = stick_breaking(q_sb, k_all, v_all, past + jnp.arange(s_new), sb_b)
    k_ext = jnp.concatenate([k_win, k_dl.astype(k_win.dtype)], axis=1)
    v_ext = jnp.concatenate([v_win, v_dl.astype(v_win.dtype)], axis=1)
    res = [dilated_sample(q_dl, k_ext, v_ext, slopes, w, r) for (w, r) in DILATIONS]
    o_dl = combine_by_denominator([a for a, _ in res], [c for _, c in res])
    m = mix_out(o_sb, g_sb, o_dl, g_dl, sb_w, dl_w, w_out)
    y = x + rmsnorm(m, post_w).astype(x.dtype)
    keep = min(MAX_WINDOW, past + s_new)
    return y, k_sb, v_sb, k_ext[:, -keep:], v_ext[:, -keep:]

def setup_inputs(seed: int = 0) -> dict:
    key = jax.random.key(seed)
    ks = jax.random.split(key, 16)
    n_pages = PAST_LEN // PAGE_SIZE
    n_used = DEC_BATCH * n_pages
    n_pool = (5 * n_used + 3) // 4
    w_buf = min(MAX_WINDOW, PAST_LEN)
    nrm = lambda k, shp: jax.random.normal(k, shp, dtype=F32)
    page_table = jax.random.permutation(ks[0], n_pool)[:n_used].reshape(DEC_BATCH, n_pages).astype(jnp.int32)
    return {
        'x_prompt': nrm(ks[1], (BATCH, SEQ, D_MODEL)),
        'x_sample': nrm(ks[2], (DEC_BATCH, DEC_SEQ, D_MODEL)),
        'cache_k_sb': nrm(ks[3], (DEPTH, n_pool, PAGE_SIZE, N_HEADS_SB, HEAD_DIM)),
        'cache_v_sb': nrm(ks[4], (DEPTH, n_pool, PAGE_SIZE, N_HEADS_SB, HEAD_DIM)),
        'cache_k_dil': nrm(ks[5], (DEPTH, DEC_BATCH, w_buf, N_HEADS_DIL, HEAD_DIM)),
        'cache_v_dil': nrm(ks[6], (DEPTH, DEC_BATCH, w_buf, N_HEADS_DIL, HEAD_DIM)),
        'page_table': page_table,
        'pre_norm_w': 1.0 + 0.1 * nrm(ks[7], (DEPTH, D_MODEL)),
        'w_in': nrm(ks[8], (DEPTH, D_MODEL, 4 * D_SB + 4 * D_DIL)) * D_MODEL ** -0.5,
        'sb_bias': SB_BIAS_INIT + 0.1 * nrm(ks[13], (DEPTH, N_HEADS_SB)),
        'sb_norm_w': 1.0 + 0.1 * nrm(ks[9], (DEPTH, D_SB)),
        'dil_norm_w': 1.0 + 0.1 * nrm(ks[10], (DEPTH, D_DIL)),
        'w_out': nrm(ks[11], (DEPTH, D_MIX, D_MODEL)) * D_MIX ** -0.5,
        'post_norm_w': 1.0 + 0.1 * nrm(ks[12], (DEPTH, D_MODEL)),
    }

def reference(x_prompt, x_sample, cache_k_sb, cache_v_sb, cache_k_dil, cache_v_dil, page_table,
              pre_norm_w, w_in, sb_bias, sb_norm_w, dil_norm_w, w_out, post_norm_w):
    slopes = alibi_slopes(N_HEADS_DIL)
    yp, ys = x_prompt, x_sample
    ksp, vsp, kss, vss, kdp, vdp, kds, vds = [], [], [], [], [], [], [], []
    for l in range(DEPTH):
        yp, a, b, c, d = prompt_layer(yp, slopes, pre_norm_w[l], w_in[l], sb_bias[l], sb_norm_w[l],
                                      dil_norm_w[l], w_out[l], post_norm_w[l])
        ksp.append(a); vsp.append(b); kdp.append(c); vdp.append(d)
        ys, a, b, c, d = sample_layer(ys, cache_k_sb[l], cache_v_sb[l], cache_k_dil[l], cache_v_dil[l],
                                      page_table, slopes, pre_norm_w[l], w_in[l], sb_bias[l], sb_norm_w[l],
                                      dil_norm_w[l], w_out[l], post_norm_w[l])
        kss.append(a); vss.append(b); kds.append(c); vds.append(d)
    return (yp, ys, jnp.stack(ksp), jnp.stack(vsp), jnp.stack(kss), jnp.stack(vss),
            jnp.stack(kdp), jnp.stack(vdp), jnp.stack(kds), jnp.stack(vds))


_drawn_inputs = setup_inputs


def setup_inputs(seed=0):
    import zlib

    import numpy as np

    out = dict(_drawn_inputs(seed))
    spreads = {}
    factors = {'sb_bias': 8.0}
    for name, (base, spread) in spreads.items():
        noise = np.random.default_rng([zlib.crc32(name.encode()), seed]).standard_normal(out[name].shape)
        drawn = base * np.exp(spread * noise) if base else spread * noise
        out[name] = __import__('jax').numpy.asarray(drawn.astype(out[name].dtype))
    for name, factor in factors.items():
        out[name] = (out[name] * factor).astype(out[name].dtype)
    return out
```

```python
import concourse.bass as bass
from concourse import mybir
from contextlib import ExitStack

F32 = mybir.dt.float32
F32R = mybir.dt.float32r
I32 = mybir.dt.int32
ACT = mybir.ActivationFunctionType
ALU = mybir.AluOpType
AX = mybir.AxisListType

P = 128
D = 1024
NK = D // P
HD = 64
NPAIR = 4
SEQ = 1024
NSAMP = 64
DB, DS = 8, 8
TOK = SEQ + NSAMP
NBLK = SEQ // P
EPS = 1e-6
SCALE = HD ** -0.5
BIG = 1e30
EXP_LN_SET = 6
EXP_CAP = 2.0 ** 60

CHUNKS = [(0, 384, 384), (384, 384, 384), (768, 256, 320)]
GROUPS = [("K", 0), ("K", 1), ("TK", 0), ("K", 2), ("TK", 1), ("V", 0), ("TK", 2), ("V", 1), ("TV", 0),
          ("V", 2), ("TV", 1), ("Q", 0), ("TV", 2), ("Q", 1), ("Q", 2), ("G", 0), ("G", 1), ("G", 2)]
NG = len(GROUPS)
TILE = {"K": 0, "V": 1, "Q": 2, "G": 3}
TILE_COL = {"Q": 0, "K": 512, "V": 1024, "G": 1536}
GIDX = {g: n for n, g in enumerate(GROUPS)}
UNITS = [(n, k) for n, (kind, _) in enumerate(GROUPS) for k in range(1 if kind[0] == "T" else NK)]
NU = len(UNITS)

SB_STEPS = [(c, kb, h) for c in range(2) for kb in range(4 * c + 3, -1, -1) for h in range(2)]
NSB = len(SB_STEPS)
DL_STEPS = []
for _h in range(2):
    for _g in range(2):
        DL_STEPS += [("score", _h, _g, _n) for _n in range(4 * _g, 4 * _g + 4)]
        DL_STEPS += [("keys", _h, _g, _kb) for _kb in range(4 * _g + 4)]
NDL = len(DL_STEPS)
P_OFF = [0, 640, 1408, 2304]
P_LEN = 3328


def share(slot, slots, part=None):
    a, b = slot * NU // slots, (slot + 1) * NU // slots
    m = a + (b - a) // 3
    return UNITS[a:b] if part is None else UNITS[a:m] if part == 0 else UNITS[m:b]


def finished(units):
    return [n for n, k in units if k == (0 if GROUPS[n][0][0] == "T" else NK - 1)]


def hymba_step(nc, x_prompt, x_sample, cache_k_sb, cache_v_sb, cache_k_dil, cache_v_dil, page_table,
               pre_norm_w, w_in, sb_bias, sb_norm_w, dil_norm_w, w_out, post_norm_w,
               c_square, c_prompt_table, c_sample_table, c_sample_mask,
               y_prompt, y_sample, k_sb_p, v_sb_p, k_sb_s, v_sb_s, k_dl_p, v_dl_p, k_dl_s, v_dl_s):
    stack = ExitStack()
    with stack:
        main = ExitStack()

        def sb(name, shape, dt=F32, ctx=stack):
            return ctx.enter_context(nc.sbuf_tensor(name, shape, dt))

        def sem(name):
            return stack.enter_context(nc.semaphore(name))

        gated = sb("gated", [P, 8, SEQ])
        samp = sb("samp", [P, 8, 3, NSAMP])
        consts = sb("consts", [P, 4, P])
        ident, head_mean, tri_f, comp_f = (consts[:, n, :] for n in range(4))
        diag_mask = sb("diag_mask", [P, P])
        bias_all = sb("bias_all", [P, 8])
        norm_w = sb("norm_w", [P, 8])
        eps_c = sb("eps_c", [P, 1])
        small = sb("small", [P, 24])
        h_hi = sb("h_hi", [P, NK, TOK], F32R, main)
        h_lo = sb("h_lo", [P, NK, TOK], F32R, main)
        w_raw = sb("w_raw", [P, 2, 4, P], F32, main)
        w_hi = sb("w_hi", [P, 2, NK, P], F32R, main)
        w_lo = sb("w_lo", [P, 2, NK, P], F32R, main)
        q_hi = sb("q_hi", [P, 2, SEQ], F32R, main)
        q_lo = sb("q_lo", [P, 2, SEQ], F32R, main)
        k_hi = sb("k_hi", [P, 2, SEQ], F32R, main)
        k_lo = sb("k_lo", [P, 2, SEQ], F32R, main)
        v_st = sb("v_st", [P, 2, NBLK, 4, HD], F32R, main)
        tri = sb("tri", [P, 2, P], F32R, main)
        work = sb("work", [P, P_LEN + 1024], F32, main)
        split = sb("split", [P, 4, 2, 512], F32R, main)
        head_t = sb("head_t", [P, SEQ], F32, main)
        fold_t = sb("fold_t", [P, 512], F32, main)
        turn = sb("turn", [P, 2, 384], F32, main)
        stage = sb("stage", [P, 2, 3, P], F32, main)
        x_in = work[:, 0:2048].rearrange("p (b n) -> p b n", b=2)
        pre_row = work[:, 2048:3072]
        junk = head_t
        z = work[:, 0:1024].rearrange("p (b n) -> p b n", b=2)
        soft = work[:, 1024:2048].rearrange("p (b n) -> p b n", b=2)
        s_hi, s_lo, a_hi, a_lo = (split[:, n] for n in range(4))
        prob = work[:, 0:P_LEN]
        table = work[:, P_LEN:P_LEN + 1024]
        pt_hi, pt_lo = a_hi, a_lo
        square = work[:, 0:1024]
        rstd_t = work[:, 1024:2048]
        main.close()
        wo_hi = sb("wo_hi", [P, 8, D], F32R)
        wo_lo = sb("wo_lo", [P, 8, D], F32R)
        wo_raw = sb("wo_raw", [P, 2, D])
        kc = sb("kc", [P, 16, P])
        vc = sb("vc", [P, 16, P])
        kct = sb("kct", [P, 16, P])
        v_new = sb("v_new", [NSAMP, P])
        q_bd = sb("q_bd", [P, 2, NSAMP])
        k_s = sb("k_s", [P, NSAMP])
        zs = sb("zs", [P, 3, P])
        es = sb("es", [P, 3, P])
        us = sb("us", [P, 3, P])
        s_table = sb("s_table", [P, 3, P])
        s_mask = sb("s_mask", [NSAMP, NSAMP])
        o_s = sb("o_s", [P, NSAMP])
        g_s = sb("g_s", [P, NSAMP])
        t_s = sb("t_s", [P, 2, NSAMP])
        gated_s = sb("gated_s", [P, 8, P])
        y_hi = sb("y_hi", [P, 2, 8, P], F32R)
        y_lo = sb("y_lo", [P, 2, 8, P], F32R)
        x_out = sb("x_out", [P, 2, D])
        m_out = sb("m_out", [P, 2, D])
        post_row = sb("post_row", [P, D])
        ones_f = sb("ones_f", [P, P])
        pages = sb("pages", [1, 16], I32)

        ps = [stack.enter_context(nc.psum_tensor(n, s, F32)) for n, s in
              (("proj_bank", [P, 2, 512]), ("sc_bank", [P, 4, 512]), ("o_bank", [P, 2, 512]))]
        proj_bank, sc_bank, o_bank = ps

        consts_in = sem("consts_in")
        consts_set = sem("consts_set")
        x_loaded = [sem(f"x_loaded{b}") for b in range(2)]
        x_sum = sem("x_sum")
        x_scaled = sem("x_scaled")
        x_turned = sem("x_turned")
        hh_set = sem("hh_set")
        hl_set = sem("hl_set")
        w_loaded = [sem(f"w_loaded{b}") for b in range(2)]
        w_hi_set = sem("w_hi_set")
        w_set = sem("w_set")
        proj_done = sem("proj_done")
        proj_hi = sem("proj_hi")
        proj_free = sem("proj_free")
        gate_step = sem("gate_step")
        turn_set = sem("turn_set")
        stage_v = sem("stage_v")
        stage_out = [sem(f"stage_out{b}") for b in range(2)]
        phase_over = sem("phase_over")
        bias_set = sem("bias_set")
        sb_scores = sem("sb_scores")
        sb_z = sem("sb_z")
        sb_exp = sem("sb_exp")
        sb_cap = sem("sb_cap")
        sb_ln = sem("sb_ln")
        sb_soft = sem("sb_soft")
        sb_shi = sem("sb_shi")
        sb_slo = sem("sb_slo")
        sb_sum = sem("sb_sum")
        sb_comp = sem("sb_comp")
        sb_u = sem("sb_u")
        sb_a = sem("sb_a")
        sb_ahi = sem("sb_ahi")
        sb_alo = sem("sb_alo")
        sb_pv = sem("sb_pv")
        table_in = sem("table_in")
        dl_scores = sem("dl_scores")
        dl_min = sem("dl_min")
        dl_exp = sem("dl_exp")
        dl_rec = sem("dl_rec")
        dl_prob = sem("dl_prob")
        dl_turned = sem("dl_turned")
        dl_hi = sem("dl_hi")
        dl_lo = sem("dl_lo")
        dl_pv = sem("dl_pv")
        fold_hi = sem("fold_hi")
        folded = sem("folded")
        squared = sem("squared")
        meaned = sem("meaned")
        rooted = sem("rooted")
        normed = sem("normed")
        wo_in = [sem(f"wo_in{b}") for b in range(2)]
        wo_hi_set = sem("wo_hi_set")
        wo_set = sem("wo_set")
        pages_in = sem("pages_in")
        kv_in = sem("kv_in")
        kct_turned = sem("kct_turned")
        kct_set = sem("kct_set")
        qbd_set = sem("qbd_set")
        s_pe = sem("s_pe")
        s_act = sem("s_act")
        s_dve = sem("s_dve")
        s_over = sem("s_over")
        yh_set = sem("yh_set")
        yl_set = sem("yl_set")
        out_done = sem("out_done")
        out_root = sem("out_root")
        out_norm = sem("out_norm")
        out_sum = sem("out_sum")
        x2_in = [sem(f"x2_in{b}") for b in range(2)]
        y_out = [sem(f"y_out{b}") for b in range(2)]
        held = {e: sem(f"held_{e}") for e in ("sp", "dve", "pool")}
        rows_out = sem("rows_out")

        w_view = w_in.rearrange("l (k p) n -> p (l k) n", p=P)
        wo_view = w_out.rearrange("l (e p) n -> p (l e) n", p=P)
        xp = x_prompt.rearrange("b t d -> (b t) d")
        xs = x_sample.rearrange("b t d -> (b t) d")
        yp = y_prompt.rearrange("b t d -> (b t) d")
        ys = y_sample.rearrange("b t d -> (b t) d")
        rows_p = {0: [t.rearrange("l b t h d -> (l b t) (h d)") for t in (k_sb_p, v_sb_p)],
                  1: [t.rearrange("l b t h d -> (l b t) (h d)") for t in (k_dl_p, v_dl_p)]}
        win = cache_k_dil.shape[2]
        rows_s = {0: [t.rearrange("l b t h d -> (l b) t (h d)") for t in (k_sb_s, v_sb_s)],
                  1: [t.rearrange("l b t h d -> (l b) t (h d)")[:, win:win + DS, :] for t in (k_dl_s, v_dl_s)]}
        pool_rows = [t.rearrange("l g p h d -> (l g) p (h d)") for t in (cache_k_sb, cache_v_sb)]
        n_pool = pool_rows[0].shape[0]
        win_rows = [t.rearrange("l b t h d -> (l b) t (h d)") for t in (cache_k_dil, cache_v_dil)]
        win_out = [t.rearrange("l b t h d -> (l b) t (h d)") for t in (k_dl_s, v_dl_s)]

        def hold(eng, name):
            eng.sem_inc(held[name], 1)

        def mix(br, i):
            return bass.ds(i + 4 * br, 1) if not isinstance(i, int) else slice(i + 4 * br, i + 4 * br + 1)

        block = stack.enter_context(nc.Block())

        @block.sync
        def _(sp):
            N_CONST = 7

            def load_half(ph, br, i, t, h):
                kind = [k for k, v in TILE.items() if v == t][0]
                n = 8 * ph + 2 * t + h
                if not (isinstance(n, int) and n < 2):
                    sp.wait_ge(w_set, n - 1)
                col = i * P + (4 * 512 * br + TILE_COL[kind])
                src = w_view[:, 4 * h:4 * h + 4, bass.ds(col, P)]
                sp.dma_start(w_raw[:, h], src).then_inc(w_loaded[h], 16)

            def store_rows(ph, br, i, kind, j):
                kv = 0 if kind == "TK" else 1
                m = 3 * kv + j
                if kv == 0:
                    sp.wait_ge(proj_free, NG * ph + GIDX[("TK", j)] + 1)
                else:
                    sp.wait_ge(stage_v, 3 * ph + j + 1)
                hold(sp, "sp")
                c0, n_p, _ = CHUNKS[j]
                nb = n_p // P
                cols = bass.ds(i * P, P)
                dst = rows_p[br][kv][c0:c0 + n_p, cols].rearrange("(b p) c -> p b c", p=P)
                sp.dma_start(dst, stage[:, m % 2, 0:nb, :]).then_inc(stage_out[m % 2], 16)
                if j == 2:
                    dst = rows_s[br][kv][:, :, cols]
                    sp.dma_start(dst, stage[0:NSAMP, m % 2, 2, :]).then_inc(stage_out[m % 2], 16)

            def projection_traffic(ph, br, i, nxt):
                for kind, j in GROUPS:
                    if kind[0] == "T":
                        store_rows(ph, br, i, kind, j)
                    elif j == 2 and TILE[kind] < 2:
                        for h in range(2):
                            load_half(ph, br, i, TILE[kind] + 2, h)
                    elif j == 2 and nxt is not None:
                        for h in range(2):
                            load_half(ph + 1, nxt[0], nxt[1], TILE[kind] - 2, h)

            sp.dma_start(x_in[:, 0], xp[0:P]).then_inc(x_loaded[0], 16)
            sp.dma_start(pre_row, pre_norm_w[0:1, :].to_broadcast((P, D))).then_inc(consts_in, 16)
            sp.dma_start(consts[:], c_square[:, 0:4, :]).then_inc(consts_in, 16)
            sp.dma_start(x_in[:, 1], xp[P:2 * P]).then_inc(x_loaded[1], 16)
            sp.dma_start(diag_mask[:], c_square[:, 5, :]).then_inc(consts_in, 16)
            sp.dma_start(bias_all[:], sb_bias[0:1, :].to_broadcast((P, 8))).then_inc(consts_in, 16)
            with nc.allow_non_contiguous_dma(reason="eight columns of norm weights"):
                sp.dma_start(norm_w[:, 0:4], sb_norm_w.rearrange("l (e p) -> p (l e)", p=P)).then_inc(consts_in, 16)
                sp.dma_start(norm_w[:, 4:8], dil_norm_w.rearrange("l (e p) -> p (l e)", p=P)).then_inc(consts_in, 16)
            for h in range(2):
                sp.dma_start(w_raw[:, h], w_view[:, 4 * h:4 * h + 4, TILE_COL["K"]:TILE_COL["K"] + P]).then_inc(w_loaded[h], 16)
            for t in range(2, 9):
                sp.wait_ge(x_scaled, t - 1)
                sp.wait_ge(hl_set, 2 * (t - 1))
                src = xp[t * P:(t + 1) * P] if t < 8 else xs
                sp.dma_start(x_in[0:src.shape[0], t % 2], src).then_inc(x_loaded[t % 2], 16)
            for h in range(2):
                load_half(0, 0, 0, 1, h)
            projection_traffic(0, 0, 0, (1, 0))

            def body(i, last):
                projection_traffic(2 * i + 1, 1, i, None if last else (0, i + 1))
                if not last:
                    projection_traffic(2 * i + 2, 0, i + 1, (1, i + 1))

            with sp.Fori(0, NPAIR - 1) as i:
                body(i, False)
            body(NPAIR - 1, True)

            for kv in range(2):
                sp.dma_start(win_out[kv][:, 0:win, :], win_rows[kv]).then_inc(rows_out, 16)
            for b in range(2):
                sp.wait_ge(stage_out[b], 64 * 8)
            sp.wait_ge(phase_over, 9)
            sp.dma_start(pages[:], page_table.rearrange("b g -> (b g)").rearrange("(a n) -> a n", a=1)).then_inc(pages_in, 16)
            sp.dma_start(s_mask[:], c_sample_mask).then_inc(pages_in, 16)
            sp.dma_start(post_row[:], post_norm_w[0:1, :].to_broadcast((P, D))).then_inc(pages_in, 16)
            for b in range(2):
                sp.dma_start(wo_raw[:, b], wo_view[:, b, :]).then_inc(wo_in[b], 16)
            sp.wait_ge(pages_in, 48)

            def sample_loads(i):
                cols = bass.ds(i * P, P)
                sp.wait_ge(s_over, 2 * i + 1)
                hold(sp, "sp")
                for n in range(16):
                    page = sp.value_load(pages[0:1, n:n + 1], min_val=0, max_val=n_pool - 1)
                    for kv, dst in ((0, kc), (1, vc)):
                        src = pool_rows[kv][bass.ds(page, 1), :, cols].rearrange("a p c -> (a p) c")
                        sp.dma_start(dst[:, n, :], src).then_inc(kv_in, 16)
                sp.dma_start(v_new[:], rows_s[0][1][:, :, cols]).then_inc(kv_in, 16)
                sp.wait_ge(s_over, 2 * i + 2)
                hold(sp, "sp")
                for kv, dst in ((0, kc), (1, vc)):
                    for b in range(DB):
                        src = win_rows[kv][b, :, cols].rearrange("(g p) c -> p g c", p=P)
                        sp.dma_start(dst[:, 2 * b:2 * b + 2, :], src).then_inc(kv_in, 16)
                sp.dma_start(v_new[:], rows_s[1][1][:, :, cols]).then_inc(kv_in, 16)
                sp.dma_start(s_table[:], c_sample_table[bass.ds(i, 1)].rearrange("a p x n -> (a p) x n")).then_inc(kv_in, 16)

            with sp.Fori(0, NPAIR) as i:
                sample_loads(i)

            for e in range(2, 8):
                sp.wait_ge(wo_set, e - 1)
                sp.dma_start(wo_raw[:, e % 2], wo_view[:, e, :]).then_inc(wo_in[e % 2], 16)
            for t in range(9):
                rows = P if t < 8 else NSAMP
                if t >= 2:
                    sp.wait_ge(out_sum, t - 1)
                src = xp[t * P:(t + 1) * P] if t < 8 else xs
                sp.dma_start(x_out[0:rows, t % 2], src).then_inc(x2_in[t % 2], 16)
                if t >= 1:
                    sp.wait_ge(out_sum, t)
                    sp.dma_start(yp[(t - 1) * P:t * P], m_out[:, (t - 1) % 2]).then_inc(y_out[(t - 1) % 2], 16)
            sp.wait_ge(out_sum, 9)
            sp.dma_start(ys, m_out[0:NSAMP, 0]).then_inc(y_out[0], 16)
            sp.wait_ge(y_out[0], 16 * 5)
            sp.wait_ge(y_out[1], 16 * 4)
            sp.wait_ge(rows_out, 32)

        @block.tensor
        def _(pe):
            mm = nc.tensor.matmul

            def project(ph, br, units):
                for n, k in units:
                    kind, j = GROUPS[n]
                    out = proj_bank[:, n % 2, :]
                    g = NG * ph + n
                    if k == 0 and not (isinstance(g, int) and g < 2):
                        pe.wait_ge(proj_free, g - 1)
                    c0, n_p, n_all = CHUNKS[j]
                    if kind[0] == "T":
                        m = j + (3 if kind == "TV" else 0)
                        if kind == "TK":
                            pe.wait_ge(turn_set, 3 * ph + j + 1)
                            pe.wait_ge(proj_free, NG * ph + GIDX[("K", j)] + 1)
                        else:
                            pe.wait_ge(proj_free, NG * ph + GIDX[("V", j)] + 1)
                        for b in range(3):
                            rows = P if P * (b + 1) <= n_p else NSAMP
                            last = mm(out[0:rows, b * P:b * P + P], turn[:, m % 2, b * P:b * P + rows], ident,
                                      start=True, stop=True, is_transpose=True)
                        last.then_inc(proj_done, 1)
                        continue
                    t = TILE[kind]
                    if k == 0 and j == 0:
                        pe.wait_ge(w_set, 8 * ph + 2 * t + 2)
                    o = out[:, 0:n_all]
                    s = t % 2
                    mm(o, w_hi[:, s, k, :], h_hi[:, k, c0:c0 + n_all], start=(k == 0), stop=False)
                    mm(o, w_hi[:, s, k, :], h_lo[:, k, c0:c0 + n_all], start=False, stop=False)
                    last = mm(o, w_lo[:, s, k, :], h_hi[:, k, c0:c0 + n_all], start=False, stop=(k == NK - 1))
                    if k == NK - 1:
                        last.then_inc(proj_done, 1)

            def mean(i2):
                pe.wait_ge(squared, i2 + 1)
                for c in range(2):
                    last = mm(sc_bank[:, 2 + c, :], head_mean, square[:, c * 512:c * 512 + 512], start=True, stop=True)
                last.then_inc(meaned, 1)

            pe.wait_ge(consts_in, 16 * 6)
            for t in range(9):
                rows = P if t < 8 else NSAMP
                pe.wait_ge(x_scaled, t + 1)
                for half in range(2):
                    n = 2 * t + half
                    if n >= 4:
                        pe.wait_ge(hl_set, n - 3)
                    for b in range(4):
                        k = 4 * half + b
                        last = mm(sc_bank[:, n % 4, b * P:b * P + rows], x_in[0:rows, t % 2, k * P:k * P + P],
                                  ident[0:rows, 0:rows], start=True, stop=True, is_transpose=True)
                    last.then_inc(x_turned, 1)
            pe.wait_ge(hl_set, 18)
            project(0, 0, UNITS)

            def sb_score(i, s):
                c, kb, h = SB_STEPS[s]
                q0 = max(512 * c, P * kb)
                n = 512 * (c + 1) - q0
                r = slice(HD * h, HD * h + HD)
                if s >= 2:
                    pe.wait_ge(sb_z, NSB * i + s - 1)
                o = sc_bank[:, h, 0:n]
                mm(o, k_hi[r, 0, kb * P:kb * P + P], q_hi[r, 0, q0:q0 + n], start=True, stop=False)
                mm(o, k_hi[r, 0, kb * P:kb * P + P], q_lo[r, 0, q0:q0 + n], start=False, stop=False)
                mm(o, k_lo[r, 0, kb * P:kb * P + P], q_hi[r, 0, q0:q0 + n], start=False, stop=True).then_inc(sb_scores, 1)

            def sb_carry(i, s):
                c, kb, h = SB_STEPS[s]
                if kb == 0:
                    return
                o0 = max(0, P * kb - 512 * c)
                pe.wait_ge(sb_u, NSB * i + s + 1)
                for part in (s_hi, s_lo):
                    last = mm(sc_bank[:, 2 + h, o0:512], tri[:, 1, :], part[:, s % 2, 0:512 - o0],
                              start=False, stop=False, skip_group_check=True)
                last.then_inc(sb_comp, 1)

            def sb_triangle(i, s):
                c, kb, h = SB_STEPS[s]
                o0 = max(0, P * kb - 512 * c)
                if kb == 4 * c + 3 and c == 1:
                    pe.wait_ge(sb_u, NSB * i + 7 + h)
                pe.wait_ge(sb_shi, NSB * i + s + 1)
                mm(sc_bank[:, 2 + h, o0:512], tri[:, 0, :], s_hi[:, s % 2, 0:512 - o0],
                   start=(kb == 4 * c + 3), stop=False, skip_group_check=True)
                pe.wait_ge(sb_slo, NSB * i + s + 1)
                mm(sc_bank[:, 2 + h, o0:512], tri[:, 0, :], s_lo[:, s % 2, 0:512 - o0],
                   start=False, stop=True, skip_group_check=True).then_inc(sb_sum, 1)

            def sb_values(i, s):
                c, kb, h = SB_STEPS[s]
                o0 = max(0, P * kb - 512 * c)
                if kb == 4 * c + 3 and c == 1:
                    pe.wait_ge(folded, 8 * i + 1 + h)
                pe.wait_ge(sb_alo, NSB * i + s + 1)
                st = v_st[:, 0, kb, 2 * h:2 * h + 2, :].rearrange("p a d -> p (a d)")
                mm(o_bank[:, h, o0:512], st, a_hi[:, s % 2, 0:512 - o0], start=(kb == 4 * c + 3), stop=False,
                   skip_group_check=True)
                mm(o_bank[:, h, o0:512], st, a_lo[:, s % 2, 0:512 - o0], start=False, stop=True,
                   skip_group_check=True).then_inc(sb_pv, 1)

            def stick_breaking(i, ph):
                slots = NSB + 2
                project(ph, 1, share(0, slots))
                pe.wait_ge(phase_over, 2 * i + 1)
                pe.wait_ge(proj_free, NG * (2 * i + 1))
                sb_score(i, 0)
                for s in range(NSB):
                    if s + 1 < NSB:
                        sb_score(i, s + 1)
                    if s >= 1:
                        sb_carry(i, s - 1)
                    project(ph, 1, share(s + 1, slots, 0))
                    sb_triangle(i, s)
                    project(ph, 1, share(s + 1, slots, 1))
                    if s >= 1:
                        sb_values(i, s - 1)
                sb_values(i, NSB - 1)
                project(ph, 1, share(NSB + 1, slots))
                mean(2 * i)

            def dl_score(i, step, n_done):
                _, h, g, n = step
                r = slice(HD * h, HD * h + HD)
                pair = 2 * (n % 2)
                if n_done >= 2:
                    pe.wait_ge(dl_min, 16 * i + n_done - 1)
                for c in range((n + 4) // 4):
                    w = min(512, P * (n + 1) - 512 * c)
                    o = sc_bank[:, pair + c, 0:w]
                    kk = slice(512 * c, 512 * c + w)
                    qq = slice(P * n, P * n + P)
                    mm(o, q_hi[r, 1, qq], k_hi[r, 1, kk], start=True, stop=False)
                    mm(o, q_hi[r, 1, qq], k_lo[r, 1, kk], start=False, stop=False)
                    last = mm(o, q_lo[r, 1, qq], k_hi[r, 1, kk], start=False, stop=True)
                last.then_inc(dl_scores, 1)

            def dl_turn(i, step, k_done, n_done):
                _, h, g, kb = step
                pe.wait_ge(dl_prob, 16 * i + n_done)
                if k_done >= 2:
                    pe.wait_ge(dl_lo, 24 * i + k_done - 1)
                for n in range(max(kb, 4 * g), 4 * g + 4):
                    q = n - 4 * g
                    last = mm(sc_bank[:, 2 * (kb % 2), q * P:q * P + P], prob[:, P_OFF[q] + kb * P:P_OFF[q] + kb * P + P],
                              ident, start=True, stop=True, is_transpose=True)
                last.then_inc(dl_turned, 1)

            def dl_values(i, step, k_done):
                _, h, g, kb = step
                b = g % 2
                if kb == 0 and (h, g) != (0, 0) and h == 1:
                    pe.wait_ge(folded, 8 * i + 4 + 1 + g)
                o0 = P * (max(kb, 4 * g) - 4 * g)
                pe.wait_ge(dl_lo, 24 * i + k_done + 1)
                st = v_st[:, 1, kb, 2 * h:2 * h + 2, :].rearrange("p a d -> p (a d)")
                mm(o_bank[:, b, o0:512], st, pt_hi[:, kb % 2, o0:512], start=(kb == 0), stop=False, skip_group_check=True)
                mm(o_bank[:, b, o0:512], st, pt_lo[:, kb % 2, o0:512], start=False, stop=True,
                   skip_group_check=True).then_inc(dl_pv, 1)

            def dilated(i, ph, fill):
                slots = NDL + 2
                if fill:
                    project(ph, 0, share(0, slots))
                pe.wait_ge(phase_over, 2 * i + 2)
                pe.wait_ge(proj_free, NG * (2 * i + 2))
                n_done = k_done = 0
                before = None
                for s, step in enumerate(DL_STEPS):
                    if step[0] == "score":
                        if before is not None:
                            dl_values(i, before, k_done - 1)
                            before = None
                        if step[3] == 0 or step[3] == 4:
                            if k_done:
                                pe.wait_ge(dl_lo, 24 * i + k_done)
                        dl_score(i, step, n_done)
                        n_done += 1
                    else:
                        dl_turn(i, step, k_done, n_done)
                        if before is not None:
                            dl_values(i, before, k_done - 1)
                        before = step
                        k_done += 1
                    if fill:
                        project(ph, 0, share(s + 1, slots))
                dl_values(i, before, k_done - 1)
                if fill:
                    project(ph, 0, share(NDL + 1, slots))
                mean(2 * i + 1)

            with pe.Fori(0, NPAIR - 1) as i:
                stick_breaking(i, 2 * i + 1)
                dilated(i, 2 * i + 2, True)
            stick_breaking(NPAIR - 1, 2 * NPAIR - 1)
            dilated(NPAIR - 1, 0, False)

            def sample(i, br):
                j = 2 * i + br
                pe.wait_ge(kv_in, (33 + 18) * 16 * i + (33 if br == 0 else 51) * 16)
                pe.wait_ge(s_over, j + 1)
                for n in range(16):
                    last = mm(sc_bank[:, n // 4, (n % 4) * P:(n % 4) * P + P], kc[:, n, :], ident, start=True, stop=True,
                              is_transpose=True)
                last.then_inc(kct_turned, 1)
                pe.wait_ge(kct_set, j + 1)
                pe.wait_ge(qbd_set, j + 1)
                past = proj_bank[:, 0, 0:256].rearrange("p (g h b q) -> p g h b q", g=2, h=2, b=DB)
                for n in range(16):
                    mm(past[:, n % 2, :, n // 2, :], kct[:, n, :], q_bd[:, :, (n // 2) * DS:(n // 2) * DS + DS],
                       start=True, stop=True)
                mm(proj_bank[0:NSAMP, 0, 256:384], k_s[:],
                   q_bd[:].rearrange("p h n -> p (h n)"), start=True, stop=True).then_inc(s_pe, 1)
                base = 5 * j
                if br == 0:
                    pe.wait_ge(s_dve, 9 * j + 3)
                    o = sc_bank[:, 0, 0:384].rearrange("p (x n) -> p x n", x=3)
                    mm(o[:, 2, :], tri_f, es[:, 2, :], start=True, stop=True)
                    mm(o[:, 1, :], tri_f, es[:, 1, :], start=True, stop=False)
                    mm(o[:, 1, :], ones_f[:], es[:, 2, :], start=False, stop=True)
                    mm(o[:, 0, :], tri_f, es[:, 0, :], start=True, stop=False)
                    mm(o[:, 0, :], ones_f[:], es[:, 1, :], start=False, stop=False)
                    mm(o[:, 0, :], ones_f[:], es[:, 2, :], start=False, stop=True).then_inc(s_pe, 1)
                else:
                    pe.wait_ge(s_dve, 9 * j + 1)
                    for x in range(3):
                        last = mm(sc_bank[:, 0, x * P:x * P + P], zs[:, x, :], ident, start=True, stop=True, is_transpose=True)
                    last.then_inc(s_pe, 1)
                    pe.wait_ge(s_dve, 9 * j + 4)
                    for x in range(3):
                        last = mm(sc_bank[:, 1, x * P:x * P + P], es[:, x, :], ident, start=True, stop=True, is_transpose=True)
                    last.then_inc(s_pe, 1)
                if br == 0:
                    pe.wait_ge(s_act, 8 * j + 3)
                else:
                    pe.wait_ge(s_act, 8 * j + 2)
                o = o_bank[:, 0, 0:P].rearrange("p (h n) -> p h n", h=2)
                mm(o_bank[:, 0, 0:P], v_new[:], us[0:NSAMP, 2, :], start=True, stop=False, skip_group_check=True)
                for n in range(16):
                    b = n // 2
                    w = us[:, n % 2, :].rearrange("p (h n) -> p h n", h=2)[:, :, b * DS:b * DS + DS]
                    last = mm(o[:, :, b * DS:b * DS + DS], vc[:, n, :], w, start=False, stop=(n == 15), skip_group_check=True)
                last.then_inc(s_pe, 1 if br else 2)
                pe.wait_ge(s_dve, 9 * j + 6)
                mm(o_bank[:, 1, 0:NSAMP], head_mean, t_s[:, 0, :], start=True, stop=True).then_inc(s_pe, 1)

            with pe.Fori(0, NPAIR) as i:
                sample(i, 0)
                sample(i, 1)

            pe.wait_ge(wo_set, 8)
            for t in range(9):
                pe.wait_ge(yl_set, t + 1)
                if t >= 2:
                    pe.wait_ge(out_norm, t - 1)
                for n in range(2):
                    o = sc_bank[:, 2 * (t % 2) + n, :]
                    ws = slice(512 * n, 512 * n + 512)
                    for e in range(8):
                        mm(o, y_hi[:, t % 2, e, :], wo_hi[:, e, ws], start=(e == 0), stop=False)
                        mm(o, y_hi[:, t % 2, e, :], wo_lo[:, e, ws], start=False, stop=False)
                        last = mm(o, y_lo[:, t % 2, e, :], wo_hi[:, e, ws], start=False, stop=(e == 7))
                last.then_inc(out_done, 1)

        @block.scalar
        def _(act):
            av = nc.scalar.activation
            pair_of = [0]
            act.add_instruction(mybir.InstLoadActFuncSet(name=nc.get_next_instruction_name(), act_func_set_id=EXP_LN_SET,
                                                         engine=mybir.EngineType.Activation, ins=[], outs=[]))

            def evacuate(ph, br, groups):
                for n in groups:
                    kind, j = GROUPS[n]
                    c0, n_p, n_all = CHUNKS[j]
                    src = proj_bank[:, n % 2, :]
                    if kind in ("V", "TK"):
                        continue
                    act.wait_ge(proj_done, NG * ph + n + 1)
                    if kind == "K":
                        av(k_hi[:, br, c0:c0 + n_p], src[:, 0:n_p], ACT.Copy).then_inc(proj_hi, 1)
                    elif kind == "Q":
                        av(q_hi[:, br, c0:c0 + n_p], src[:, 0:n_p], ACT.Copy,
                           scale=(SCALE if br == 0 else -SCALE)).then_inc(proj_hi, 1)
                    elif kind == "G":
                        out = gated[:, mix(br, pair_of[0]), c0:c0 + n_p].rearrange("p a n -> p (a n)")
                        av(out, src[:, 0:n_p], ACT.Exp, scale=-1.0).then_inc(proj_hi, 1)
                    else:
                        m = 3 + j
                        wait_stage(ph, m)
                        nb = n_p // P
                        ins = av(stage[:, m % 2, 0:nb, :].rearrange("p b c -> p (b c)"), src[:, 0:n_p], ACT.Copy)
                        if j == 2:
                            ins = av(stage[0:NSAMP, m % 2, 2, :], src[0:NSAMP, 2 * P:3 * P], ACT.Copy)
                        ins.then_inc(stage_v, 1)
                        b0 = c0 // P
                        av(v_st[:, br, b0:b0 + nb, 0:4:3, :], src[:, 0:n_p].rearrange("p (b h d) -> p b h d", b=nb, h=2),
                           ACT.Copy).then_inc(proj_hi, 1)

            def wait_stage(ph, m):
                before = {0: 0, 1: 0, 2: 16, 3: 16, 4: 48, 5: 32}[m]
                if isinstance(ph, int) and ph == 0 and before == 0:
                    return
                act.wait_ge(stage_out[m % 2], 64 * ph + before)

            def fold(i8, bank, h, sem_pv, value):
                own, other = slice(HD * h, HD * h + HD), slice(HD * (1 - h), HD * (1 - h) + HD)
                act.wait_ge(sem_pv, value)
                act.wait_ge(folded, i8 + 1)
                av(fold_t[own, :], o_bank[other, bank, :], ACT.Copy).then_inc(fold_hi, 1)

            def root(i2):
                act.wait_ge(meaned, i2 + 1)
                av(rstd_t, sc_bank[:, 2:4, :].rearrange("p a n -> p (a n)"), ACT.Ln, bias=eps_c[:, 0:1]).then_inc(rooted, 1)
                act.wait_ge(rooted, 2 * i2 + 1)
                av(rstd_t, rstd_t, ACT.Exp, scale=-0.5).then_inc(rooted, 1)

            def load_table(head):
                act.dma_start(table, c_prompt_table[bass.ds(head, 1)].rearrange("a p n -> (a p) n")).then_inc(table_in, 16)

            load_table(0)
            act.wait_ge(consts_set, 1)
            for t in range(9):
                rows = P if t < 8 else NSAMP
                act.wait_ge(x_loaded[t % 2], 16 * (t // 2 + 1))
                if t >= 1:
                    act.wait_ge(x_scaled, t)
                av(junk[0:rows, :], x_in[0:rows, t % 2], ACT.Square, accum_out=small[0:rows, 0:1]).then_inc(x_sum, 1)
                act.wait_ge(x_sum, 3 * t + 1)
                av(small[0:rows, 1:2], small[0:rows, 0:1], ACT.Ln, scale=1.0 / D, bias=eps_c[0:rows, 0:1]).then_inc(x_sum, 1)
                act.wait_ge(x_sum, 3 * t + 2)
                av(small[0:rows, 2:3], small[0:rows, 1:2], ACT.Exp, scale=-0.5).then_inc(x_sum, 1)
                for half in range(2):
                    n = 2 * t + half
                    act.wait_ge(x_turned, n + 1)
                    av(h_hi[:, 4 * half:4 * half + 4, t * P:t * P + rows],
                       sc_bank[:, n % 4, :].rearrange("p (b n) -> p b n", b=4)[:, :, 0:rows], ACT.Copy).then_inc(hh_set, 1)
            evacuate(0, 0, range(NG))

            def stick_breaking(i, ph):
                slots = NSB + 2
                b0 = NSB * i
                pair_of[0] = i
                evacuate(ph, 1, finished(share(0, slots)))
                act.wait_ge(phase_over, 2 * i + 1)

                def width(s):
                    c, kb, h = SB_STEPS[s]
                    return 512 * (c + 1) - max(512 * c, P * kb)

                def exp_z(s):
                    if s >= 2:
                        act.wait_ge(sb_slo, b0 + s - 1)
                    act.wait_ge(sb_z, b0 + s + 1)
                    av(soft[:, s % 2, 0:width(s)], z[:, s % 2, 0:width(s)], ACT.Exp).then_inc(sb_exp, 1)

                def ln(s):
                    act.wait_ge(sb_cap, b0 + s + 1)
                    av(soft[:, s % 2, 0:width(s)], soft[:, s % 2, 0:width(s)], ACT.Ln).then_inc(sb_ln, 1)

                def s_high(s):
                    act.wait_ge(sb_soft, b0 + s + 1)
                    if s >= 2:
                        act.wait_ge(sb_sum, b0 + s - 1)
                        c2 = sum(1 for t in range(s - 1) if SB_STEPS[t][1] > 0)
                        if c2:
                            act.wait_ge(sb_comp, 20 * i + c2)
                    av(s_hi[:, s % 2, 0:width(s)], soft[:, s % 2, 0:width(s)], ACT.Copy).then_inc(sb_shi, 1)

                exp_z(0)
                ln(0)
                s_high(0)
                for s in range(NSB):
                    w = width(s)
                    if s + 1 < NSB:
                        exp_z(s + 1)
                    evacuate(ph, 1, finished(share(s + 1, slots, 0)))
                    act.wait_ge(sb_u, b0 + s + 1)
                    av(z[:, s % 2, 0:w], z[:, s % 2, 0:w], ACT.Exp).then_inc(sb_a, 1)
                    if s + 1 < NSB:
                        ln(s + 1)
                    act.wait_ge(sb_a, b0 + s + 1)
                    if s >= 2:
                        act.wait_ge(sb_pv, b0 + s - 1)
                    av(a_hi[:, s % 2, 0:w], z[:, s % 2, 0:w], ACT.Copy).then_inc(sb_ahi, 1)
                    if s + 1 < NSB:
                        s_high(s + 1)
                    evacuate(ph, 1, finished(share(s + 1, slots, 1)))
                    if s >= 1 and SB_STEPS[s - 1][1] == 0:
                        c, _, h = SB_STEPS[s - 1]
                        fold(8 * i + 2 * c + h - 0, h, h, sb_pv, b0 + s)
                fold(8 * i + 3, 1, 1, sb_pv, b0 + NSB)
                evacuate(ph, 1, finished(share(NSB + 1, slots)))
                root(2 * i)

            def dilated(i, ph, fill):
                slots = NDL + 2
                pair_of[0] = i + 1
                if fill:
                    evacuate(ph, 0, finished(share(0, slots)))
                act.wait_ge(phase_over, 2 * i + 2)
                n_done = k_done = 0
                for s, (kind, h, g, x) in enumerate(DL_STEPS):
                    if kind == "score":
                        q, length = x % 4, P * (x + 1)
                        act.wait_ge(dl_min, 16 * i + n_done + 1)
                        row = prob[:, P_OFF[q]:P_OFF[q] + length]
                        av(row, row, ACT.Exp, scale=-1.0, bias=small[:, 4 + q:5 + q],
                           accum_out=small[:, 8 + q:9 + q]).then_inc(dl_exp, 1)
                        n_done += 1
                        if n_done == 8:
                            load_table(2 * i + 1)
                        elif n_done == 16 and fill:
                            load_table(2 * i + 2)
                    else:
                        o0 = P * (max(x, 4 * g) - 4 * g)
                        act.wait_ge(dl_turned, 24 * i + k_done + 1)
                        if k_done >= 2:
                            act.wait_ge(dl_pv, 24 * i + k_done - 1)
                        av(pt_hi[:, x % 2, o0:512], sc_bank[:, 2 * (x % 2), o0:512], ACT.Copy).then_inc(dl_hi, 1)
                        k_done += 1
                    if fill:
                        evacuate(ph, 0, finished(share(s + 1, slots)))
                    if kind == "score" and x % 4 == 0 and n_done > 1:
                        pg = 1 - g
                        ph_ = h if g == 1 else h - 1
                        fold(8 * i + 4 + 2 * ph_ + pg, pg, ph_, dl_pv, 24 * i + k_done)
                fold(8 * i + 7, 1, 1, dl_pv, 24 * i + 24)
                if fill:
                    evacuate(ph, 0, finished(share(NDL + 1, slots)))
                root(2 * i + 1)

            with act.Fori(0, NPAIR - 1) as i:
                stick_breaking(i, 2 * i + 1)
                dilated(i, 2 * i + 2, True)
            stick_breaking(NPAIR - 1, 2 * NPAIR - 1)
            dilated(NPAIR - 1, 0, False)

            def sample(i, br):
                j = 2 * i + br
                act.wait_ge(kct_turned, j + 1)
                av(kct[:].rearrange("p n c -> p (n c)"), sc_bank[:].rearrange("p a n -> p (a n)"), ACT.Copy).then_inc(kct_set, 1)
                if br == 0:
                    act.wait_ge(s_dve, 9 * j + 1)
                    av(es[:], zs[:], ACT.Exp).then_inc(s_act, 1)
                    act.wait_ge(s_dve, 9 * j + 2)
                    av(es[:], es[:], ACT.Ln).then_inc(s_act, 1)
                    act.wait_ge(s_dve, 9 * j + 4)
                    av(us[:], us[:], ACT.Exp).then_inc(s_act, 1)
                else:
                    act.wait_ge(s_dve, 9 * j + 2)
                    av(es[:].rearrange("p x n -> p (x n)"), sc_bank[:, 0, 0:384], ACT.Exp, scale=-1.0,
                       bias=small[:, 4:5], accum_out=small[:, 8:9]).then_inc(s_act, 1)
                    act.wait_ge(s_pe, 5 * j + 3)
                    av(us[:].rearrange("p x n -> p (x n)"), sc_bank[:, 1, 0:384], ACT.Copy).then_inc(s_act, 2)
                gate = samp[:, mix(br, i), 2, :].rearrange("p a n -> p (a n)")
                av(g_s[:], gate, ACT.Exp, scale=-1.0).then_inc(s_act, 1)
                act.wait_ge(s_pe, 5 * j + 5)
                av(t_s[:, 1, :], o_bank[:, 1, 0:NSAMP], ACT.Ln, bias=eps_c[:, 0:1]).then_inc(s_act, 1)
                act.wait_ge(s_act, 8 * j + 5)
                av(t_s[:, 1, :], t_s[:, 1, :], ACT.Exp, scale=-0.5).then_inc(s_act, 3)

            with act.Fori(0, NPAIR) as i:
                sample(i, 0)
                sample(i, 1)

            def high(t):
                if t >= 2:
                    act.wait_ge(out_done, t - 1)
                if t == 8:
                    act.wait_ge(s_over, 9)
                src = gated[:, :, t * P:(t + 1) * P] if t < 8 else gated_s[:]
                av(y_hi[:, t % 2], src, ACT.Copy).then_inc(yh_set, 1)

            high(0)
            high(1)
            for t in range(9):
                act.wait_ge(out_done, t + 1)
                if t >= 2:
                    act.wait_ge(y_out[t % 2], 16 * (t // 2))
                bank = sc_bank[:, 2 * (t % 2):2 * (t % 2) + 2, :].rearrange("p a n -> p (a n)")
                av(m_out[:, t % 2], bank, ACT.Square, accum_out=small[:, 12 + 4 * (t % 2):13 + 4 * (t % 2)]).then_inc(out_root, 1)
                act.wait_ge(out_root, 3 * t + 1)
                c = 12 + 4 * (t % 2)
                av(small[:, c + 1:c + 2], small[:, c:c + 1], ACT.Ln, scale=1.0 / D, bias=eps_c[:, 0:1]).then_inc(out_root, 1)
                act.wait_ge(out_root, 3 * t + 2)
                av(small[:, c + 2:c + 3], small[:, c + 1:c + 2], ACT.Exp, scale=-0.5).then_inc(out_root, 1)
                if t + 2 < 9:
                    high(t + 2)

        @block.vector
        def _(dve):
            ve = nc.vector

            def evacuate(ph, br, groups):
                for n in groups:
                    kind, j = GROUPS[n]
                    c0, n_p, n_all = CHUNKS[j]
                    src = proj_bank[:, n % 2, :]
                    own = {g: m for m, g in enumerate([g for g in GROUPS if g[0] not in ("V", "TK")])}
                    i = pair_of[0]
                    tail = src[:, n_p:n_all]

                    def kept(x):
                        return samp[:, mix(br, i), x, :].rearrange("p a n -> p (a n)")

                    if (kind, j) in own:
                        dve.wait_ge(proj_hi, len(own) * ph + own[(kind, j)] + 1)
                    else:
                        dve.wait_ge(proj_done, NG * ph + n + 1)
                    if kind == "K":
                        ins = ve.tensor_tensor(k_lo[:, br, c0:c0 + n_p], src[:, 0:n_p], k_hi[:, br, c0:c0 + n_p].bitcast(F32),
                                               ALU.subtract)
                        if j == 2:
                            ve.tensor_copy(kept(1), tail)
                            ins = ve.tensor_copy(turn[:, j % 2, n_p:n_all], tail)
                        ins.then_inc(proj_free, 1)
                    elif kind == "Q":
                        c = SCALE if br == 0 else -SCALE
                        ins = ve.scalar_tensor_tensor(q_lo[:, br, c0:c0 + n_p], src[:, 0:n_p], c,
                                                      q_hi[:, br, c0:c0 + n_p].bitcast(F32), ALU.mult, ALU.subtract)
                        if j == 2:
                            ins = ve.tensor_scalar(kept(0), tail, c, None, ALU.mult)
                        ins.then_inc(proj_free, 1)
                    elif kind == "V":
                        ve.tensor_copy(turn[:, (3 + j) % 2, 0:n_all], src[:, 0:n_all]).then_inc(proj_free, 1)
                    elif kind == "G":
                        st = 2 * (3 * ph + j)
                        out = gated[:, mix(br, i), c0:c0 + n_p].rearrange("p a n -> p (a n)")
                        ve.tensor_scalar(out, out, 1.0, None, ALU.add).then_inc(gate_step, 1)
                        dve.wait_ge(gate_step, st + 1)
                        hold(dve, "dve")
                        ve.reciprocal(out, out).then_inc(gate_step, 1)
                        dve.wait_ge(gate_step, st + 2)
                        ins = ve.tensor_tensor(out, src[:, 0:n_p], out, ALU.mult)
                        if j == 2:
                            ins = ve.tensor_copy(kept(2), tail)
                        ins.then_inc(proj_free, 1)
                    elif kind == "TK":
                        before = {0: 0, 1: 0, 2: 16}[j]
                        if not (isinstance(ph, int) and ph == 0 and before == 0):
                            dve.wait_ge(stage_out[j % 2], 64 * ph + before)
                        nb = n_p // P
                        ins = ve.tensor_copy(stage[:, j % 2, 0:nb, :].rearrange("p b c -> p (b c)"), src[:, 0:n_p])
                        if j == 2:
                            ins = ve.tensor_copy(stage[0:NSAMP, j % 2, 2, :], src[0:NSAMP, 2 * P:3 * P])
                        ins.then_inc(proj_free, 1)
                    else:
                        nb, b0 = n_p // P, c0 // P
                        ve.tensor_tensor(v_st[:, br, b0:b0 + nb, 1:3, :],
                                         src[:, 0:n_p].rearrange("p (b h d) -> p b h d", b=nb, h=2),
                                         v_st[:, br, b0:b0 + nb, 0:4:3, :].bitcast(F32), ALU.subtract).then_inc(proj_free, 1)

            pair_of = [0]

            def fold(i8, bank, h, c):
                own = slice(HD * h, HD * h + HD)
                dve.wait_ge(fold_hi, i8 + 1)
                ve.tensor_tensor(head_t[own, c * 512:c * 512 + 512], o_bank[own, bank, :], fold_t[own, :], ALU.add)\
                    .then_inc(folded, 1)

            def gate(i, br, i2):
                dve.wait_ge(rooted, 2 * i2 + 2)
                ve.tensor_tensor(head_t[:], head_t[:], rstd_t, ALU.mult).then_inc(normed, 1)
                dve.wait_ge(normed, i2 + 1)
                y = gated[:, mix(br, i), :].rearrange("p a n -> p (a n)")
                w = norm_w[:, mix(br, i)]
                ve.scalar_tensor_tensor(y, head_t[:], w, y, ALU.mult, ALU.mult).then_inc(phase_over, 1)

            ve.memset(eps_c[:], EPS).then_inc(consts_set, 1)
            dve.wait_ge(consts_in, 16 * 6)
            ve.tensor_copy(tri[:], consts[:, 2:4, :]).then_inc(consts_set, 1)
            for t in range(9):
                rows = P if t < 8 else NSAMP
                dve.wait_ge(x_sum, 3 * t + 3)
                ve.scalar_tensor_tensor(x_in[0:rows, t % 2], x_in[0:rows, t % 2], small[0:rows, 2:3], pre_row[0:rows, :],
                                        ALU.mult, ALU.mult).then_inc(x_scaled, 1)
                for half in range(2):
                    n = 2 * t + half
                    dve.wait_ge(hh_set, n + 1)
                    dst = (slice(None), slice(4 * half, 4 * half + 4), slice(t * P, t * P + rows))
                    ve.tensor_tensor(h_lo[dst], sc_bank[:, n % 4, :].rearrange("p (b n) -> p b n", b=4)[:, :, 0:rows],
                                     h_hi[dst].bitcast(F32), ALU.subtract).then_inc(hl_set, 1)
            evacuate(0, 0, range(NG))
            ve.memset(fold_t[0:1, 0:1], 0.0).then_inc(phase_over, 1)
            ve.memset(fold_t[0:1, 1:2], 0.0).then_inc(folded, 1)

            def stick_breaking(i, ph):
                slots = NSB + 2
                b0 = NSB * i
                pair_of[0] = i
                evacuate(ph, 1, finished(share(0, slots)))
                ve.tensor_copy(small[:, 20:22], bias_all[:, bass.ds(i * 2, 2)]).then_inc(bias_set, 1)
                dve.wait_ge(bias_set, i + 1)

                def shape(s):
                    c, kb, h = SB_STEPS[s]
                    o0 = max(0, P * kb - 512 * c)
                    return c, kb, h, o0, 512 - o0

                def shift(s):
                    c, kb, h, o0, w = shape(s)
                    b = small[:, 20 + h:21 + h]
                    dve.wait_ge(sb_scores, b0 + s + 1)
                    zz, src = z[:, s % 2, :], sc_bank[:, h, :]
                    if s >= 2:
                        dve.wait_ge(sb_alo, b0 + s - 1)
                    if kb >= 4 * c:
                        ins = ve.scalar_tensor_tensor(zz[:, 0:P], src[:, 0:P], b, diag_mask[:], ALU.add, ALU.add)
                        if w > P:
                            ins = ve.tensor_scalar(zz[:, P:w], src[:, P:w], b, None, ALU.add)
                    else:
                        ins = ve.tensor_scalar(zz[:, 0:w], src[:, 0:w], b, None, ALU.add)
                    ins.then_inc(sb_z, 1)

                def cap(s):
                    w = shape(s)[4]
                    dve.wait_ge(sb_exp, b0 + s + 1)
                    ve.tensor_scalar(soft[:, s % 2, 0:w], soft[:, s % 2, 0:w], EXP_CAP, 1.0, ALU.min, ALU.add).then_inc(sb_cap, 1)

                def softplus(s):
                    w = shape(s)[4]
                    dve.wait_ge(sb_ln, b0 + s + 1)
                    ve.tensor_tensor(soft[:, s % 2, 0:w], soft[:, s % 2, 0:w], z[:, s % 2, 0:w], ALU.max).then_inc(sb_soft, 1)

                shift(0)
                cap(0)
                softplus(0)
                for s in range(NSB):
                    c, kb, h, o0, w = shape(s)
                    if s + 1 < NSB:
                        shift(s + 1)
                    evacuate(ph, 1, finished(share(s + 1, slots, 0)))
                    dve.wait_ge(sb_sum, b0 + s + 1)
                    dve.wait_ge(sb_soft, b0 + s + 1)
                    ve.tensor_tensor(z[:, s % 2, 0:w], z[:, s % 2, 0:w], sc_bank[:, 2 + h, o0:512], ALU.subtract).then_inc(sb_u, 1)
                    if s + 1 < NSB:
                        cap(s + 1)
                        softplus(s + 1)
                    dve.wait_ge(sb_ahi, b0 + s + 1)
                    if s >= 2:
                        dve.wait_ge(sb_pv, b0 + s - 1)
                    ve.tensor_tensor(a_lo[:, s % 2, 0:w], z[:, s % 2, 0:w], a_hi[:, s % 2, 0:w].bitcast(F32), ALU.subtract)\
                        .then_inc(sb_alo, 1)
                    evacuate(ph, 1, finished(share(s + 1, slots, 1)))
                    if s >= 1 and SB_STEPS[s - 1][1] == 0:
                        cc, _, hh = SB_STEPS[s - 1]
                        fold(8 * i + 2 * cc + hh, hh, hh, cc)
                fold(8 * i + 3, 1, 1, 1)
                evacuate(ph, 1, finished(share(NSB + 1, slots)))
                gate(i, 0, 2 * i)

            def dilated(i, ph, fill):
                slots = NDL + 2
                pair_of[0] = i + 1
                if fill:
                    evacuate(ph, 0, finished(share(0, slots)))
                n_done = k_done = 0
                for s, (kind, h, g, x) in enumerate(DL_STEPS):
                    if kind == "score":
                        q, length = x % 4, P * (x + 1)
                        dve.wait_ge(dl_scores, 16 * i + n_done + 1)
                        if x == 0:
                            dve.wait_ge(table_in, 32 * i + 16 * h + 16)
                        if k_done:
                            dve.wait_ge(dl_turned, 24 * i + k_done)
                        bank = sc_bank[:, 2 * (x % 2):2 * (x % 2) + 2, :].rearrange("p a n -> p (a n)")
                        row = prob[:, P_OFF[q]:P_OFF[q] + length]
                        hold(dve, "dve")
                        ve.tensor_tensor_reduce(out=row, in0=bank[:, 0:length], in1=table[:, 1024 - length:1024],
                                                scale=1.0, scalar=3.0 * BIG, op0=ALU.add, op1=ALU.min,
                                                accum_out=small[:, 4 + q:5 + q]).then_inc(dl_min, 1)
                        if fill:
                            evacuate(ph, 0, finished(share(s + 1, slots)))
                        dve.wait_ge(dl_exp, 16 * i + n_done + 1)
                        ve.reciprocal(small[:, 8 + q:9 + q], small[:, 8 + q:9 + q]).then_inc(dl_rec, 1)
                        dve.wait_ge(dl_rec, 16 * i + n_done + 1)
                        ve.tensor_scalar(row, row, small[:, 8 + q:9 + q], None, ALU.mult).then_inc(dl_prob, 1)
                        n_done += 1
                    else:
                        o0 = P * (max(x, 4 * g) - 4 * g)
                        dve.wait_ge(dl_hi, 24 * i + k_done + 1)
                        ve.tensor_tensor(pt_lo[:, x % 2, o0:512], sc_bank[:, 2 * (x % 2), o0:512],
                                         pt_hi[:, x % 2, o0:512].bitcast(F32), ALU.subtract).then_inc(dl_lo, 1)
                        k_done += 1
                        if fill:
                            evacuate(ph, 0, finished(share(s + 1, slots)))
                    if kind == "score" and x % 4 == 0 and n_done > 1:
                        pg = 1 - g
                        ph_ = h if g == 1 else h - 1
                        fold(8 * i + 4 + 2 * ph_ + pg, pg, ph_, pg)
                fold(8 * i + 7, 1, 1, 1)
                if fill:
                    evacuate(ph, 0, finished(share(NDL + 1, slots)))
                gate(i, 1, 2 * i + 1)

            with dve.Fori(0, NPAIR - 1) as i:
                stick_breaking(i, 2 * i + 1)
                dilated(i, 2 * i + 2, True)
            stick_breaking(NPAIR - 1, 2 * NPAIR - 1)
            dilated(NPAIR - 1, 0, False)

            dve.wait_ge(phase_over, 9)
            ve.memset(q_bd[:], 0.0).then_inc(consts_set, 1)
            ve.memset(gated_s[:], 0.0).then_inc(consts_set, 1)
            ve.memset(ones_f[:], 1.0).then_inc(consts_set, 1)
            dve.wait_ge(consts_set, 5)
            dve.wait_ge(pages_in, 48)
            ve.memset(zs[HD:P, 2, :], -BIG).then_inc(s_over, 1)

            def sample(i, br):
                j = 2 * i + br
                d = 9 * j
                q = samp[:, mix(br, i), 0, :].rearrange("p a n -> p (a n)")
                if br == 0:
                    dve.wait_ge(s_over, j + 1)
                ve.tensor_copy(k_s[:], samp[:, mix(br, i), 1, :].rearrange("p a n -> p (a n)"))
                ve.tensor_copy(q_bd[0:HD, 0, :], q[0:HD])
                ve.tensor_copy(q_bd[HD:P, 1, :], q[HD:P]).then_inc(qbd_set, 1)
                past, new = proj_bank[:, 0, 0:256], proj_bank[0:NSAMP, 0, 256:384]
                dve.wait_ge(s_pe, 5 * j + 1)
                if br == 0:
                    ve.memset(zs[HD:P, 2, :], -BIG)
                    ve.tensor_copy(small[:, 20:22], bias_all[:, bass.ds(i * 2, 2)]).then_inc(bias_set, 1)
                    dve.wait_ge(bias_set, NPAIR + i + 1)
                    for h in range(2):
                        b = small[:, 20 + h:21 + h]
                        hs = slice(h * HD, h * HD + HD)
                        ve.tensor_scalar(zs[:, 0:2, hs], past.rearrange("p (g n) -> p g n", g=2)[:, :, hs], b, None, ALU.add)
                        ins = ve.scalar_tensor_tensor(zs[0:NSAMP, 2, hs], new[:, hs], b[0:NSAMP], s_mask[:], ALU.add, ALU.add)
                    ins.then_inc(s_dve, 1)
                    dve.wait_ge(s_act, 8 * j + 1)
                    ve.tensor_scalar(es[:], es[:], EXP_CAP, 1.0, ALU.min, ALU.add).then_inc(s_dve, 1)
                    dve.wait_ge(s_act, 8 * j + 2)
                    dve.wait_ge(s_dve, d + 1)
                    ve.tensor_tensor(es[:], es[:], zs[:], ALU.max).then_inc(s_dve, 1)
                    dve.wait_ge(s_pe, 5 * j + 2)
                    ve.tensor_tensor(us[:].rearrange("p x n -> p (x n)"), zs[:].rearrange("p x n -> p (x n)"),
                                     sc_bank[:, 0, 0:384], ALU.subtract).then_inc(s_dve, 1)
                else:
                    dve.wait_ge(kv_in, 51 * 16 * i + 51 * 16)
                    ve.memset(zs[HD:P, 2, :], BIG)
                    ve.tensor_tensor(zs[:, 0:2, :].rearrange("p x n -> p (x n)"), past,
                                     s_table[:, 0:2, :].rearrange("p x n -> p (x n)"), ALU.add)
                    ve.tensor_tensor(zs[0:NSAMP, 2, :], new, s_table[0:NSAMP, 2, :], ALU.add).then_inc(s_dve, 1)
                    dve.wait_ge(s_pe, 5 * j + 2)
                    ve.tensor_reduce(small[:, 4:5], sc_bank[:, 0, 0:384], AX.X, ALU.min).then_inc(s_dve, 1)
                    dve.wait_ge(s_act, 8 * j + 1)
                    ve.reciprocal(small[:, 8:9], small[:, 8:9]).then_inc(s_dve, 1)
                    dve.wait_ge(s_dve, d + 3)
                    ve.tensor_scalar(es[:], es[:], small[:, 8:9], None, ALU.mult).then_inc(s_dve, 1)
                dve.wait_ge(s_pe, 5 * j + 4)
                ve.tensor_copy(o_s[0:HD], o_bank[0:HD, 0, 0:HD])
                ve.tensor_copy(o_s[HD:P], o_bank[HD:P, 0, HD:P]).then_inc(s_dve, 1)
                dve.wait_ge(s_dve, d + 5)
                ve.tensor_tensor(t_s[:, 0, :], o_s[:], o_s[:], ALU.mult).then_inc(s_dve, 1)
                dve.wait_ge(s_act, 8 * j + 4)
                gate_in = samp[:, mix(br, i), 2, :].rearrange("p a n -> p (a n)")
                ve.tensor_scalar(g_s[:], g_s[:], 1.0, None, ALU.add).then_inc(s_dve, 1)
                dve.wait_ge(s_dve, d + 7)
                ve.reciprocal(g_s[:], g_s[:]).then_inc(s_dve, 1)
                dve.wait_ge(s_dve, d + 8)
                ve.tensor_tensor(g_s[:], g_s[:], gate_in, ALU.mult)
                dve.wait_ge(s_act, 8 * j + 8)
                ve.tensor_tensor(o_s[:], o_s[:], t_s[:, 1, :], ALU.mult).then_inc(s_dve, 1)
                dve.wait_ge(s_dve, d + 9)
                out = gated_s[:, mix(br, i), 0:NSAMP].rearrange("p a n -> p (a n)")
                ve.scalar_tensor_tensor(out, o_s[:], norm_w[:, mix(br, i)], g_s[:], ALU.mult, ALU.mult).then_inc(s_over, 1)

            with dve.Fori(0, NPAIR) as i:
                sample(i, 0)
                sample(i, 1)

            for t in range(9):
                dve.wait_ge(out_root, 3 * t + 3)
                c = 12 + 4 * (t % 2)
                bank = sc_bank[:, 2 * (t % 2):2 * (t % 2) + 2, :].rearrange("p a n -> p (a n)")
                ve.scalar_tensor_tensor(m_out[:, t % 2], bank, small[:, c + 2:c + 3], post_row[:], ALU.mult, ALU.mult)\
                    .then_inc(out_norm, 1)

        @block.gpsimd
        def _(pool):
            gp = nc.gpsimd

            def split_tile(ph, t):
                n = 4 * ph + t
                order = [GIDX[(kind, 2)] for kind in TILE]
                if t >= 2:
                    pool.wait_ge(proj_done, NG * ph + order[t - 2] + 1)
                elif not (isinstance(ph, int) and ph == 0):
                    pool.wait_ge(proj_done, NG * ph - NG + order[t + 2] + 1)
                for h in range(2):
                    pool.wait_ge(w_loaded[h], 16 * n + 16)
                    ks = slice(4 * h, 4 * h + 4)
                    hold(pool, "pool")
                    gp.tensor_copy(w_hi[:, t % 2, ks, :], w_raw[:, h]).then_inc(w_hi_set, 1)
                    pool.wait_ge(w_hi_set, 2 * n + h + 1)
                    gp.tensor_tensor(w_lo[:, t % 2, ks, :], w_raw[:, h], w_hi[:, t % 2, ks, :].bitcast(F32), ALU.subtract)\
                        .then_inc(w_set, 1)

            def evacuate(ph, br, groups, nxt):
                for n in groups:
                    kind, j = GROUPS[n]
                    c0, n_p, _ = CHUNKS[j]
                    if kind == "K":
                        pool.wait_ge(proj_free, NG * ph + n + 1)
                        gp.tensor_tensor(turn[:, j % 2, 0:n_p], k_hi[:, br, c0:c0 + n_p].bitcast(F32),
                                         k_lo[:, br, c0:c0 + n_p].bitcast(F32), ALU.add).then_inc(turn_set, 1)
                    if kind in TILE and j == 2:
                        if TILE[kind] < 2:
                            split_tile(ph, TILE[kind] + 2)
                        elif nxt:
                            split_tile(ph + 1, TILE[kind] - 2)

            def squares(i2):
                pool.wait_ge(folded, 4 * i2 + 5)
                gp.tensor_tensor(square, head_t[:], head_t[:], ALU.mult).then_inc(squared, 1)

            split_tile(0, 0)
            split_tile(0, 1)
            evacuate(0, 0, range(NG), True)

            def stick_breaking(i, ph, nxt):
                slots = NSB + 2
                b0 = NSB * i
                evacuate(ph, 1, finished(share(0, slots)), nxt)

                def s_low(s):
                    c, kb, h = SB_STEPS[s]
                    w = 512 * (c + 1) - max(512 * c, P * kb)
                    pool.wait_ge(sb_shi, b0 + s + 1)
                    gp.tensor_tensor(s_lo[:, s % 2, 0:w], soft[:, s % 2, 0:w], s_hi[:, s % 2, 0:w].bitcast(F32), ALU.subtract)\
                        .then_inc(sb_slo, 1)

                s_low(0)
                for s in range(NSB):
                    evacuate(ph, 1, finished(share(s + 1, slots, 0)), nxt)
                    if s + 1 < NSB:
                        s_low(s + 1)
                    evacuate(ph, 1, finished(share(s + 1, slots, 1)), nxt)
                evacuate(ph, 1, finished(share(NSB + 1, slots)), nxt)
                squares(2 * i)

            def dilated(i, ph, fill):
                slots = NDL + 2
                if fill:
                    for s in range(slots):
                        evacuate(ph, 0, finished(share(s, slots)), True)
                squares(2 * i + 1)

            with pool.Fori(0, NPAIR - 1) as i:
                stick_breaking(i, 2 * i + 1, True)
                dilated(i, 2 * i + 2, True)
            stick_breaking(NPAIR - 1, 2 * NPAIR - 1, False)
            dilated(NPAIR - 1, 0, False)

            pool.wait_ge(phase_over, 9)
            for e in range(8):
                pool.wait_ge(wo_in[e % 2], 16 * (e // 2 + 1))
                gp.tensor_copy(wo_hi[:, e, :], wo_raw[:, e % 2]).then_inc(wo_hi_set, 1)
                pool.wait_ge(wo_hi_set, e + 1)
                gp.tensor_tensor(wo_lo[:, e, :], wo_raw[:, e % 2], wo_hi[:, e, :].bitcast(F32), ALU.subtract).then_inc(wo_set, 1)

            def low(t):
                pool.wait_ge(yh_set, t + 1)
                src = gated[:, :, t * P:(t + 1) * P] if t < 8 else gated_s[:]
                gp.tensor_tensor(y_lo[:, t % 2], src, y_hi[:, t % 2].bitcast(F32), ALU.subtract).then_inc(yl_set, 1)

            low(0)
            low(1)
            for t in range(9):
                rows = P if t < 8 else NSAMP
                pool.wait_ge(out_norm, t + 1)
                pool.wait_ge(x2_in[t % 2], 16 * (t // 2 + 1))
                gp.tensor_tensor(m_out[0:rows, t % 2], m_out[0:rows, t % 2], x_out[0:rows, t % 2], ALU.add).then_inc(out_sum, 1)
                if t + 2 < 9:
                    low(t + 2)


def _constants():
    import numpy as np
    k = np.arange(128)
    sq = np.zeros((128, 6, 128), np.float32)
    sq[:, 0] = np.eye(128)
    sq[:, 1] = (k[:, None] // 64 == k[None, :] // 64) / 64.0
    sq[:, 2] = k[:, None] >= k[None, :]
    sq[:, 3] = k[:, None] < k[None, :]
    sq[:, 4] = 1.0
    sq[:, 5] = np.where(k[:, None] < k[None, :], 0.0, -1e30)

    def term(dist, slope):
        n = sum((dist >= 0) & (dist % r == 0) & (dist <= w) for w, r in ((128, 1), (512, 4), (2048, 16)))
        n = n.astype(np.int64)
        return np.where(n > 0, slope * dist - np.log(np.maximum(n, 1)), 1e30).astype(np.float32)

    slopes = 2.0 ** (-np.arange(1, 9, dtype=np.float64))
    x = np.arange(1024)
    prompt = np.stack([term(k[:, None] + 896 - x[None, :], s) for s in slopes])
    sample = np.full((4, 128, 3, 2, 8, 8), 1e30, np.float32)
    q = np.arange(8)
    for p in range(4):
        for h in range(2):
            s = slopes[2 * p + h]
            for g in range(2):
                sample[p, :, g, h] = term(256 + q[None, :] - (128 * g + k[:, None]), s)[:, None, :]
            for b in range(8):
                sample[p, 8 * b:8 * b + 8, 2, h, b] = term(q[None, :] - q[:, None], s)
    mask = np.full((64, 8, 8), -1e30, np.float32)
    for b in range(8):
        mask[8 * b:8 * b + 8, b] = np.where(q[:, None] < q[None, :], 0.0, -1e30)
    return {"c_square": sq, "c_prompt_table": prompt, "c_sample_table": sample.reshape(4, 128, 3, 128),
            "c_sample_mask": mask.reshape(64, 64)}


_INS = ["x_prompt", "x_sample", "cache_k_sb", "cache_v_sb", "cache_k_dil", "cache_v_dil", "page_table", "pre_norm_w",
        "w_in", "sb_bias", "sb_norm_w", "dil_norm_w", "w_out", "post_norm_w"]
_OUTS = [(1, 1024, 1024), (8, 8, 1024), (1, 1, 1024, 8, 64), (1, 1, 1024, 8, 64), (1, 8, 8, 8, 64), (1, 8, 8, 8, 64),
         (1, 1, 1024, 8, 64), (1, 1, 1024, 8, 64), (1, 8, 264, 8, 64), (1, 8, 264, 8, 64)]


def kernel(**inputs):
    import numpy as _np
    import concourse.bacc as _bacc
    from concourse import mybir as _mybir
    from concourse.bass_utils import run_bass_kernel_spmd as _run

    nc = _bacc.Bacc("TRN2", target_bir_lowering=False, num_devices=1, dynamic_dma_scratch_size=1024)
    arrays, args = {}, []
    given = {n: _np.ascontiguousarray(inputs[n]) for n in _INS}
    given.update(_constants())
    for name, a in given.items():
        arrays[f"in_{name}_dram"] = a
        args.append(nc.dram_tensor(f"in_{name}_dram", a.shape, _mybir.dt.from_np(a.dtype), kind="ExternalInput").ap())
    for i, shape in enumerate(_OUTS):
        args.append(nc.dram_tensor(f"out_{i}_dram", shape, _mybir.dt.float32, kind="ExternalOutput").ap())
    hymba_step(nc, *args)
    r = _run(nc, [arrays], core_ids=[0])
    return tuple(r.results[0][f"out_{i}_dram"] for i in range(len(_OUTS)))
```

```python
import concourse.bass as bass
from concourse import mybir
from contextlib import ExitStack

F32 = mybir.dt.float32
F32R = mybir.dt.float32r
I32 = mybir.dt.int32
ACT = mybir.ActivationFunctionType
ALU = mybir.AluOpType
AX = mybir.AxisListType

P = 128
D = 1024
NK = D // P
HD = 64
NPAIR = 4
SEQ = 1024
NSAMP = 64
DB, DS = 8, 8
TOK = SEQ + NSAMP
NBLK = SEQ // P
EPS = 1e-6
SCALE = HD ** -0.5
FAR = 1e30
LINEAR = 40.0
EXP_LN_SET = 6

CHUNKS = [(0, 384, 384), (384, 384, 384), (768, 256, 320)]
TILE = {"K": 0, "V": 1, "Q": 2, "G": 3}
TILE_COL = {"Q": 0, "K": 512, "V": 1024, "G": 1536}
KINDS = list(TILE)


def _units(order):
    return [(g, k) for g in order for k in range(NK if g[0] in TILE else 1)]


UNITS = (_units([("K", 0), ("M", 0), ("K", 1), ("TK", 0)]) + [(("K", 2), k) for k in range(4)] + [(("M", 1), 0)]
         + [(("K", 2), k) for k in range(4, NK)]
         + _units([("TK", 1), ("V", 0), ("TK", 2), ("V", 1), ("TV", 0), ("V", 2), ("TV", 1), ("Q", 0), ("TV", 2),
                   ("Q", 1), ("Q", 2), ("G", 0), ("G", 1), ("G", 2)]))
UNITS_FIRST = [u for u in UNITS if u[0][0] != "M"]
UNITS_LAST = [(("M", 0), 0)] + [None] * 5 + [(("M", 1), 0)] + [None] * 37


def _order(units, small):
    out = []
    for u in units:
        if u and (u[0][0] not in TILE) == small and u[0] not in out:
            out.append(u[0])
    return out


BIG = _order(UNITS, False)
SMALL = _order(UNITS, True)
SMALL_FIRST = _order(UNITS_FIRST, True)
NBIG, NSMALL = len(BIG), len(SMALL)

SB_STEPS = [(c, kb, h) for c in range(2) for kb in range(4 * c + 3, -1, -1) for h in range(2)]
NSB = len(SB_STEPS)
SB_CARRIES = sum(kb > 0 for _, kb, _ in SB_STEPS)
DL_STEPS = []
for _h in range(2):
    for _g in range(2):
        DL_STEPS += [("score", _h, _g, _n) for _n in range(4 * _g, 4 * _g + 4)]
        DL_STEPS += [("keys", _h, _g, _kb) for _kb in range(4 * _g + 4)]
NDL = len(DL_STEPS)
NSCORE, NKEYS = 16, 24
P_OFF = [0, 640, 1408, 2304]
P_LEN = 3328
KV_LOADS = (33, 18)
TURN_BANK = (2, 0)
LEAD = 3


def share(units, slot, steps):
    slots, n = steps + LEAD + 1, len(units)
    a = 0 if slot < 0 else slot + LEAD
    b = slot + LEAD + 1
    return units[a * n // slots:b * n // slots]


def finished(units):
    return [u[0] for u in units if u and (u[0][0] not in TILE or u[1] == NK - 1)]


def ended(units, slot, steps):
    return finished(share(units, slot, steps)) if -1 <= slot <= steps else []


FIRST = [[g] for g in finished(UNITS_FIRST)]


def big_no(ph, group):
    return NBIG * ph + BIG.index(group)


def small_no(ph, group):
    if isinstance(ph, int) and ph == 0:
        return SMALL_FIRST.index(group)
    if isinstance(ph, int) and ph >= 8:
        return NSMALL * 8 - 2 + 2 * (ph - 8) + group[1]
    return NSMALL * ph - 2 + SMALL.index(group)


def hymba_step(nc, x_prompt, x_sample, cache_k_sb, cache_v_sb, cache_k_dil, cache_v_dil, page_table,
               pre_norm_w, w_in, sb_bias, sb_norm_w, dil_norm_w, w_out, post_norm_w,
               c_square, c_prompt_table, c_sample_table, c_sample_mask,
               y_prompt, y_sample, k_sb_p, v_sb_p, k_sb_s, v_sb_s, k_dl_p, v_dl_p, k_dl_s, v_dl_s):
    stack = ExitStack()
    with stack:
        main = ExitStack()

        def sb(name, shape, dt=F32, ctx=stack):
            return ctx.enter_context(nc.sbuf_tensor(name, shape, dt))

        def sem(name):
            return stack.enter_context(nc.semaphore(name))

        gated = sb("gated", [P, 8, SEQ])
        samp = sb("samp", [P, 8, 3, NSAMP])
        consts = sb("consts", [P, 4, P])
        ident, head_mean, tri_f, comp_f = (consts[:, n, :] for n in range(4))
        diag_mask = sb("diag_mask", [P, P])
        bias_all = sb("bias_all", [P, 8])
        norm_w = sb("norm_w", [P, 8])
        eps_c = sb("eps_c", [P, 1])
        one_c = sb("one_c", [P, 1])
        pages = sb("pages", [1, 16], I32)
        small = sb("small", [P, 24])
        h_hi = sb("h_hi", [P, NK, TOK], F32R, main)
        h_lo = sb("h_lo", [P, NK, TOK], F32R, main)
        w_raw = sb("w_raw", [P, 2, 4, P], F32, main)
        w_hi = sb("w_hi", [P, 2, NK, P], F32R, main)
        w_lo = sb("w_lo", [P, 2, NK, P], F32R, main)
        q_hi = sb("q_hi", [P, 2, SEQ], F32R, main)
        q_lo = sb("q_lo", [P, 2, SEQ], F32R, main)
        k_hi = sb("k_hi", [P, 2, SEQ], F32R, main)
        k_lo = sb("k_lo", [P, 2, SEQ], F32R, main)
        v_st = sb("v_st", [P, 2, NBLK, 4, HD], F32R, main)
        tri = sb("tri", [P, 2, P], F32R, main)
        work = sb("work", [P, P_LEN + 1024], F32, main)
        split = sb("split", [P, 4, 2, 512], F32R, main)
        head_t = sb("head_t", [P, SEQ], F32, main)
        fold_t = sb("fold_t", [P, 512], F32, main)
        turn = sb("turn", [P, 2, 384], F32, main)
        stage = sb("stage", [P, 2, 3, P], F32, main)
        x_in = [gated[:, t] for t in range(8)] + [work[:, 0:D]]
        pre_row = work[:, D:2 * D]
        junk = head_t
        z = work[:, 0:1536].rearrange("p (b n) -> p b n", b=3)
        soft = work[:, 1536:3072].rearrange("p (b n) -> p b n", b=3)
        s_hi, s_lo, a_hi, a_lo = (split[:, n] for n in range(4))
        prob = work[:, 0:P_LEN]
        table = work[:, P_LEN:P_LEN + 1024]
        pt_hi, pt_lo = a_hi, a_lo
        main.close()
        wo_hi = sb("wo_hi", [P, 8, D], F32R)
        wo_lo = sb("wo_lo", [P, 8, D], F32R)
        wo_raw = sb("wo_raw", [P, 2, D])
        kc0 = sb("kc0", [P, 16, P])
        vc0 = sb("vc0", [P, 16, P])
        kc1 = sb("kc1", [P, 16, P])
        vc1 = sb("vc1", [P, 16, P])
        kcs, vcs = (kc0, kc1), (vc0, vc1)
        kct = sb("kct", [P, 16, P])
        v_new = sb("v_new", [NSAMP, 2, P])
        q_bd = sb("q_bd", [P, 2, NSAMP])
        k_s = sb("k_s", [P, NSAMP])
        zs = sb("zs", [P, 3, P])
        es = sb("es", [P, 3, P])
        us = sb("us", [P, 3, P])
        s_table = sb("s_table", [P, 3, P])
        s_mask = sb("s_mask", [NSAMP, NSAMP])
        o_s = sb("o_s", [P, NSAMP])
        g_s = sb("g_s", [P, NSAMP])
        t_s = sb("t_s", [P, 2, NSAMP])
        gated_s = sb("gated_s", [P, 8, P])
        y_hi = sb("y_hi", [P, 2, 8, P], F32R)
        y_lo = sb("y_lo", [P, 2, 8, P], F32R)
        x_out = sb("x_out", [P, 2, D])
        m_out = sb("m_out", [P, 2, D])
        post_row = sb("post_row", [P, D])
        ones_f = sb("ones_f", [P, P])

        ps = [stack.enter_context(nc.psum_tensor(n, s, F32)) for n, s in
              (("proj_bank", [P, 2, 512]), ("sc_bank", [P, 4, 512]), ("o_bank", [P, 2, 512]))]
        proj_bank, sc_bank, o_bank = ps

        rows_in = sem("rows_in")
        consts_in = sem("consts_in")
        consts_set = sem("consts_set")
        x_loaded = [sem(f"x_loaded{t}") for t in range(9)]
        x_sum = sem("x_sum")
        x_scaled = sem("x_scaled")
        x_turned = sem("x_turned")
        hh_set = sem("hh_set")
        hl_set = sem("hl_set")
        w_loaded = [sem(f"w_loaded{b}") for b in range(2)]
        w_hi_set = sem("w_hi_set")
        w_set = sem("w_set")
        big_done = sem("big_done")
        big_free = sem("big_free")
        small_done = sem("small_done")
        small_free = sem("small_free")
        hi_set = sem("hi_set")
        gate_act = sem("gate_act")
        gate_dve = sem("gate_dve")
        turn_set = sem("turn_set")
        stage_v = sem("stage_v")
        stage_out = [sem(f"stage_out{b}") for b in range(2)]
        squared = sem("squared")
        rooted = sem("rooted")
        normed = sem("normed")
        gated_set = sem("gated_set")
        bias_set = sem("bias_set")
        sb_scores = sem("sb_scores")
        sb_z = sem("sb_z")
        sb_exp = sem("sb_exp")
        sb_cap = sem("sb_cap")
        sb_ln = sem("sb_ln")
        sb_soft = sem("sb_soft")
        sb_shi = sem("sb_shi")
        sb_slo = sem("sb_slo")
        sb_sum = sem("sb_sum")
        sb_comp = sem("sb_comp")
        sb_u = sem("sb_u")
        sb_a = sem("sb_a")
        sb_ahi = sem("sb_ahi")
        sb_alo = sem("sb_alo")
        sb_pv = sem("sb_pv")
        table_in = sem("table_in")
        dl_scores = sem("dl_scores")
        dl_min = sem("dl_min")
        dl_exp = sem("dl_exp")
        dl_rec = sem("dl_rec")
        dl_prob = sem("dl_prob")
        dl_turned = sem("dl_turned")
        dl_hi = sem("dl_hi")
        dl_lo = sem("dl_lo")
        dl_pv = sem("dl_pv")
        fold_hi = sem("fold_hi")
        folded = sem("folded")
        wo_in = [sem(f"wo_in{b}") for b in range(2)]
        wo_hi_set = sem("wo_hi_set")
        wo_set = sem("wo_set")
        pages_in = sem("pages_in")
        kv_in = [sem(f"kv_in{b}") for b in range(2)]
        kct_turned = sem("kct_turned")
        kct_set = sem("kct_set")
        qbd_set = sem("qbd_set")
        s_pe = sem("s_pe")
        s_act = sem("s_act")
        s_dve = sem("s_dve")
        s_over = sem("s_over")
        yh_set = sem("yh_set")
        yl_set = sem("yl_set")
        out_done = sem("out_done")
        out_root = sem("out_root")
        out_norm = sem("out_norm")
        out_sum = sem("out_sum")
        x2_in = [sem(f"x2_in{b}") for b in range(2)]
        y_out = [sem(f"y_out{b}") for b in range(2)]
        held = {e: sem(f"held_{e}") for e in ("sp", "act", "dve")}
        rows_out = sem("rows_out")

        w_view = w_in.rearrange("l (k p) n -> p (l k) n", p=P)
        wo_view = w_out.rearrange("l (e p) n -> p (l e) n", p=P)
        xp = x_prompt.rearrange("b t d -> (b t) d")
        xs = x_sample.rearrange("b t d -> (b t) d")
        yp = y_prompt.rearrange("b t d -> (b t) d")
        ys = y_sample.rearrange("b t d -> (b t) d")
        rows_p = {0: [t.rearrange("l b t h d -> (l b t) (h d)") for t in (k_sb_p, v_sb_p)],
                  1: [t.rearrange("l b t h d -> (l b t) (h d)") for t in (k_dl_p, v_dl_p)]}
        win = cache_k_dil.shape[2]
        rows_s = {0: [t.rearrange("l b t h d -> (l b) t (h d)") for t in (k_sb_s, v_sb_s)],
                  1: [t.rearrange("l b t h d -> (l b) t (h d)")[:, win:win + DS, :] for t in (k_dl_s, v_dl_s)]}
        pool_rows = [t.rearrange("l g p h d -> (l g) p (h d)") for t in (cache_k_sb, cache_v_sb)]
        n_pool = pool_rows[0].shape[0]
        win_rows = [t.rearrange("l b t h d -> (l b) t (h d)") for t in (cache_k_dil, cache_v_dil)]
        win_out = [t.rearrange("l b t h d -> (l b) t (h d)") for t in (k_dl_s, v_dl_s)]

        def hold(eng, name):
            eng.sem_inc(held[name], 1)

        def mix(br, i):
            return bass.ds(i + 4 * br, 1) if not isinstance(i, int) else slice(i + 4 * br, i + 4 * br + 1)

        block = stack.enter_context(nc.Block())

        @block.sync
        def _(sp):
            def load_tile(ph, br, i, kind):
                for h in range(2):
                    n = 4 * ph + TILE[kind]
                    if not (isinstance(n, int) and n < 1):
                        sp.wait_ge(w_set, 2 * n - 1 + h)
                        hold(sp, "sp")
                    col = i * P + (4 * 512 * br + TILE_COL[kind])
                    sp.dma_start(w_raw[:, h], w_view[:, 4 * h:4 * h + 4, bass.ds(col, P)]).then_inc(w_loaded[h], 16)

            def store_rows(ph, br, i, kind, j):
                kv = 0 if kind == "TK" else 1
                m = 3 * kv + j
                if kv == 0:
                    sp.wait_ge(small_free, small_no(ph, ("TK", j)) + 1)
                else:
                    sp.wait_ge(stage_v, 3 * ph + j + 1)
                hold(sp, "sp")
                c0, n_p, _ = CHUNKS[j]
                nb = n_p // P
                cols = bass.ds(i * P, P)
                dst = rows_p[br][kv][c0:c0 + n_p, cols].rearrange("(b p) c -> p b c", p=P)
                sp.dma_start(dst, stage[:, m % 2, 0:nb, :]).then_inc(stage_out[m % 2], 16)
                if j == 2:
                    dst = rows_s[br][kv][:, :, cols]
                    sp.dma_start(dst, stage[0:NSAMP, m % 2, 2, :]).then_inc(stage_out[m % 2], 16)

            def projection_traffic(ph, br, i, nxt):
                for kind, j in [u[0] for u in (UNITS_FIRST if isinstance(ph, int) and ph == 0 else UNITS)
                                if u[1] == (NK - 1 if u[0][0] in TILE else 0)]:
                    if kind in ("TK", "TV"):
                        store_rows(ph, br, i, kind, j)
                    elif kind in TILE and j == 0:
                        if TILE[kind] < 2:
                            load_tile(ph, br, i, KINDS[TILE[kind] + 2])
                        elif nxt is not None:
                            load_tile(ph + 1, nxt[0], nxt[1], KINDS[TILE[kind] - 2])

            sp.dma_start(x_in[0], xp[0:P]).then_inc(x_loaded[0], 16)
            sp.dma_start(pre_row, pre_norm_w[0:1, :].to_broadcast((P, D))).then_inc(rows_in, 16)
            sp.dma_start(consts[:], c_square[:, 0:4, :]).then_inc(rows_in, 16)
            sp.dma_start(x_in[1], xp[P:2 * P]).then_inc(x_loaded[1], 16)
            load_tile(0, 0, 0, "K")
            for t in range(2, 9):
                src = xp[t * P:(t + 1) * P] if t < 8 else xs
                sp.dma_start(x_in[t][0:src.shape[0]], src).then_inc(x_loaded[t], 16)
            sp.dma_start(diag_mask[:], c_square[:, 5, :]).then_inc(consts_in, 16)
            sp.dma_start(bias_all[:], sb_bias[0:1, :].to_broadcast((P, 8))).then_inc(consts_in, 16)
            with nc.allow_non_contiguous_dma(reason="eight columns of norm weights"):
                sp.dma_start(norm_w[:, 0:4], sb_norm_w.rearrange("l (e p) -> p (l e)", p=P)).then_inc(consts_in, 16)
                sp.dma_start(norm_w[:, 4:8], dil_norm_w.rearrange("l (e p) -> p (l e)", p=P)).then_inc(consts_in, 16)
            load_tile(0, 0, 0, "V")
            projection_traffic(0, 0, 0, (1, 0))

            def body(i, last):
                projection_traffic(2 * i + 1, 1, i, None if last else (0, i + 1))
                if not last:
                    projection_traffic(2 * i + 2, 0, i + 1, (1, i + 1))

            with sp.Fori(0, NPAIR - 1) as i:
                body(i, False)
            body(NPAIR - 1, True)

            sp.wait_ge(big_done, NBIG * 8)
            sp.wait_ge(big_free, NBIG * 8)
            for b in range(2):
                sp.wait_ge(stage_out[b], 64 * 8)
            sp.dma_start(pages[:], page_table.rearrange("b g -> (b g)").rearrange("(a n) -> a n", a=1)).then_inc(pages_in, 16)
            for b in range(2):
                sp.dma_start(wo_raw[:, b], wo_view[:, b, :]).then_inc(wo_in[b], 16)
            sp.wait_ge(pages_in, 16)

            def load_paged(i):
                cols = bass.ds(i * P, P)
                for n in range(16):
                    page = sp.value_load(pages[0:1, n:n + 1], min_val=0, max_val=n_pool - 1)
                    for kv, dst in ((0, kc0), (1, vc0)):
                        src = pool_rows[kv][bass.ds(page, 1), :, cols].rearrange("a p c -> (a p) c")
                        sp.dma_start(dst[:, n, :], src).then_inc(kv_in[0], 16)

            def load_rest(i):
                cols = bass.ds(i * P, P)
                sp.dma_start(v_new[:, 0, :], rows_s[0][1][:, :, cols]).then_inc(kv_in[0], 16)
                for kv, dst in ((0, kc1), (1, vc1)):
                    for b in range(DB):
                        src = win_rows[kv][b, :, cols].rearrange("(g p) c -> p g c", p=P)
                        sp.dma_start(dst[:, 2 * b:2 * b + 2, :], src).then_inc(kv_in[1], 16)
                sp.dma_start(v_new[:, 1, :], rows_s[1][1][:, :, cols]).then_inc(kv_in[1], 16)
                sp.dma_start(s_table[:], c_sample_table[bass.ds(i, 1)].rearrange("a p x n -> (a p) x n")).then_inc(kv_in[1], 16)

            load_paged(0)
            for e in range(2, 8):
                sp.wait_ge(wo_set, e - 1)
                sp.dma_start(wo_raw[:, e % 2], wo_view[:, e, :]).then_inc(wo_in[e % 2], 16)
            for kv in range(2):
                sp.dma_start(win_out[kv][:, 0:win, :], win_rows[kv]).then_inc(rows_out, 16)
            sp.wait_ge(folded, 4 * 8 + 1)
            load_rest(0)
            sp.dma_start(s_mask[:], c_sample_mask).then_inc(pages_in, 16)
            sp.dma_start(post_row[:], post_norm_w[0:1, :].to_broadcast((P, D))).then_inc(pages_in, 16)

            def residual_in(t, b):
                sp.dma_start(x_out[:, b], xp[bass.ds(t * P, P), :]).then_inc(x2_in[b], 16)

            for b in range(2):
                sp.sem_inc(y_out[b], 16)

            def output_rows(t, b):
                sp.wait_ge(out_sum, t + 1)
                hold(sp, "sp")
                sp.dma_start(yp[bass.ds(t * P, P), :], m_out[:, b]).then_inc(y_out[b], 16)

            def late_traffic(i, last):
                residual_in(2 * i, 0)
                residual_in(2 * i + 1, 1)
                if not last:
                    sp.wait_ge(s_over, 2 * i + 2)
                    hold(sp, "sp")
                    load_paged(i + 1)
                output_rows(2 * i, 0)
                if not last:
                    sp.wait_ge(s_over, 2 * i + 3)
                    hold(sp, "sp")
                    load_rest(i + 1)
                output_rows(2 * i + 1, 1)

            with sp.Fori(0, NPAIR - 1) as i:
                late_traffic(i, False)
            late_traffic(NPAIR - 1, True)
            sp.dma_start(x_out[0:NSAMP, 0], xs).then_inc(x2_in[0], 16)
            sp.wait_ge(out_sum, 9)
            sp.dma_start(ys, m_out[0:NSAMP, 0]).then_inc(y_out[0], 16)
            sp.wait_ge(y_out[0], 16 * 6)
            sp.wait_ge(y_out[1], 16 * 5)
            sp.wait_ge(rows_out, 32)

        @block.tensor
        def _(pe):
            mm = nc.tensor.matmul

            def project(ph, units):
                for unit in units:
                    if unit is None:
                        continue
                    (kind, j), k = unit
                    if kind not in TILE:
                        small_group(ph, kind, j)
                        continue
                    n = big_no(ph, (kind, j))
                    c0, _, n_all = CHUNKS[j]
                    bank = BIG.index((kind, j)) % 2
                    s = TILE[kind] % 2
                    if k == 0:
                        if not (isinstance(n, int) and n < 2):
                            pe.wait_ge(big_free, n - 1)
                        if j == 0:
                            pe.wait_ge(w_set, 8 * ph + 2 * TILE[kind] + 2)
                    o = proj_bank[:, bank, 0:n_all]
                    mm(o, w_hi[:, s, k, :], h_hi[:, k, c0:c0 + n_all], start=(k == 0), stop=False)
                    mm(o, w_hi[:, s, k, :], h_lo[:, k, c0:c0 + n_all], start=False, stop=False)
                    last = mm(o, w_lo[:, s, k, :], h_hi[:, k, c0:c0 + n_all], start=False, stop=(k == NK - 1))
                    if k == NK - 1:
                        last.then_inc(big_done, 1)

            def small_group(ph, kind, j):
                n = small_no(ph, (kind, j))
                if not (isinstance(n, int) and n < 1):
                    pe.wait_ge(small_free, n)
                out = sc_bank[:, 3, :]
                if kind == "M":
                    pe.wait_ge(squared, 2 * ph - 1 + j)
                    mm(out, head_mean, fold_t[:], start=True, stop=True).then_inc(small_done, 1)
                    return
                m = j + (3 if kind == "TV" else 0)
                n_p = CHUNKS[j][1]
                if kind == "TK":
                    pe.wait_ge(turn_set, 3 * ph + j + 1)
                    pe.wait_ge(big_free, big_no(ph, ("K", j)) + 1)
                else:
                    pe.wait_ge(big_free, big_no(ph, ("V", j)) + 1)
                for b in range(3):
                    rows = P if P * (b + 1) <= n_p else NSAMP
                    last = mm(out[0:rows, b * P:b * P + P], turn[:, m % 2, b * P:b * P + rows], ident,
                              start=True, stop=True, is_transpose=True)
                last.then_inc(small_done, 1)

            def turn_tokens(t, half):
                rows, n = (P if t < 8 else NSAMP), 2 * t + half
                pe.wait_ge(x_scaled, t + 1)
                if n >= 3:
                    pe.wait_ge(hl_set, n - 2)
                for b in range(4):
                    k = 4 * half + b
                    last = mm(sc_bank[:, n % 3, b * P:b * P + rows], x_in[t][0:rows, k * P:k * P + P],
                              ident[0:rows, 0:rows], start=True, stop=True, is_transpose=True)
                last.then_inc(x_turned, 1)

            pe.wait_ge(consts_set, 2)
            for t in range(9):
                j = t // 3
                if t % 3 == 0 and j > 0:
                    pe.wait_ge(hl_set, 6 * j)
                for half in range(2):
                    turn_tokens(t, half)
                    if j > 0:
                        n = 2 * (t % 3) + half
                        project(0, [(("K", j - 1), k) for k in range(n * NK // 6, (n + 1) * NK // 6)])
            pe.wait_ge(hl_set, 18)
            project(0, [u for u in UNITS_FIRST if u[0] not in (("K", 0), ("K", 1))])

            def sb_shape(s):
                c, kb, h = SB_STEPS[s]
                return c, kb, h, max(0, P * kb - 512 * c)

            def sb_score(i, s):
                c, kb, h, o0 = sb_shape(s)
                q0, n = 512 * c + o0, 512 - o0
                r = slice(HD * h, HD * h + HD)
                if s >= 1:
                    pe.wait_ge(sb_z, NSB * i + s)
                o = sc_bank[:, 0, 0:n]
                mm(o, k_hi[r, 0, kb * P:kb * P + P], q_hi[r, 0, q0:q0 + n], start=True, stop=False)
                mm(o, k_hi[r, 0, kb * P:kb * P + P], q_lo[r, 0, q0:q0 + n], start=False, stop=False)
                mm(o, k_lo[r, 0, kb * P:kb * P + P], q_hi[r, 0, q0:q0 + n], start=False, stop=True).then_inc(sb_scores, 1)

            def sb_carry(i, s):
                c, kb, h, o0 = sb_shape(s)
                if kb == 0:
                    return
                pe.wait_ge(sb_u, NSB * i + s + 1)
                for part in (s_hi, s_lo):
                    last = mm(sc_bank[:, 1 + h, o0:512], tri[:, 1, :], part[:, s % 2, 0:512 - o0],
                              start=False, stop=False, skip_group_check=True)
                last.then_inc(sb_comp, 1)

            def sb_triangle(i, s):
                c, kb, h, o0 = sb_shape(s)
                if s >= 2:
                    pe.wait_ge(sb_u, NSB * i + s - 1)
                pe.wait_ge(sb_shi, NSB * i + s + 1)
                mm(sc_bank[:, 1 + h, o0:512], tri[:, 0, :], s_hi[:, s % 2, 0:512 - o0],
                   start=(kb == 4 * c + 3), stop=False, skip_group_check=True)
                pe.wait_ge(sb_slo, NSB * i + s + 1)
                mm(sc_bank[:, 1 + h, o0:512], tri[:, 0, :], s_lo[:, s % 2, 0:512 - o0],
                   start=False, stop=True, skip_group_check=True).then_inc(sb_sum, 1)

            def sb_values(i, s):
                c, kb, h, o0 = sb_shape(s)
                if kb == 4 * c + 3 and c == 1:
                    pe.wait_ge(folded, 8 * i + 2 + h)
                pe.wait_ge(sb_alo, NSB * i + s + 1)
                st = v_st[:, 0, kb, 2 * h:2 * h + 2, :].rearrange("p a d -> p (a d)")
                mm(o_bank[:, h, o0:512], st, a_hi[:, s % 2, 0:512 - o0], start=(kb == 4 * c + 3), stop=False,
                   skip_group_check=True)
                mm(o_bank[:, h, o0:512], st, a_lo[:, s % 2, 0:512 - o0], start=False, stop=True,
                   skip_group_check=True).then_inc(sb_pv, 1)

            def stick_breaking(i, ph):
                project(ph, share(UNITS, -1, NSB))
                pe.wait_ge(folded, 8 * i + 1)
                pe.wait_ge(big_free, NBIG * ph)
                pe.wait_ge(small_free, NSMALL * ph - 2)
                sb_score(i, 0)
                sb_score(i, 1)
                for s in range(NSB):
                    sb_triangle(i, s)
                    if s >= 1:
                        sb_carry(i, s - 1)
                    if s + 2 < NSB:
                        sb_score(i, s + 2)
                    project(ph, share(UNITS, s, NSB))
                    if s >= 1:
                        sb_values(i, s - 1)
                sb_values(i, NSB - 1)
                project(ph, share(UNITS, NSB, NSB))

            def dl_score(i, step, n_done):
                _, h, g, n = step
                r = slice(HD * h, HD * h + HD)
                if n_done >= 1:
                    pe.wait_ge(dl_min, NSCORE * i + n_done)
                for c in range((n + 4) // 4):
                    w = min(512, P * (n + 1) - 512 * c)
                    o = sc_bank[:, c, 0:w]
                    kk = slice(512 * c, 512 * c + w)
                    qq = slice(P * n, P * n + P)
                    mm(o, q_hi[r, 1, qq], k_hi[r, 1, kk], start=True, stop=False)
                    mm(o, q_hi[r, 1, qq], k_lo[r, 1, kk], start=False, stop=False)
                    last = mm(o, q_lo[r, 1, qq], k_hi[r, 1, kk], start=False, stop=True)
                last.then_inc(dl_scores, 1)

            def dl_turn(i, step, k_done, n_done):
                _, h, g, kb = step
                pe.wait_ge(dl_prob, 16 * i + n_done)
                if k_done >= 2:
                    pe.wait_ge(dl_lo, 24 * i + k_done - 1)
                for n in range(max(kb, 4 * g), 4 * g + 4):
                    q = n - 4 * g
                    last = mm(sc_bank[:, TURN_BANK[kb % 2], q * P:q * P + P], prob[:, P_OFF[q] + kb * P:P_OFF[q] + kb * P + P],
                              ident, start=True, stop=True, is_transpose=True)
                last.then_inc(dl_turned, 1)

            def dl_values(i, step, k_done):
                _, h, g, kb = step
                b = g % 2
                if kb == 0 and h == 1:
                    pe.wait_ge(folded, 8 * i + 4 + 2 + g)
                o0 = P * (max(kb, 4 * g) - 4 * g)
                pe.wait_ge(dl_lo, 24 * i + k_done + 1)
                st = v_st[:, 1, kb, 2 * h:2 * h + 2, :].rearrange("p a d -> p (a d)")
                mm(o_bank[:, b, o0:512], st, pt_hi[:, kb % 2, o0:512], start=(kb == 0), stop=False, skip_group_check=True)
                mm(o_bank[:, b, o0:512], st, pt_lo[:, kb % 2, o0:512], start=False, stop=True,
                   skip_group_check=True).then_inc(dl_pv, 1)

            def dilated(i, ph, units):
                project(ph, share(units, -1, NDL))
                pe.wait_ge(folded, 8 * i + 5)
                if isinstance(ph, int) and ph == 8:
                    pe.wait_ge(big_free, NBIG * 8)
                    pe.wait_ge(small_free, NSMALL * 8 - 2)
                else:
                    pe.wait_ge(big_free, NBIG * ph)
                    pe.wait_ge(small_free, NSMALL * ph - 2)
                n_done = k_done = 0
                before = None
                for s, step in enumerate(DL_STEPS):
                    if step[0] == "score":
                        if before is not None:
                            dl_values(i, before, k_done - 1)
                            before = None
                        if step[3] % 4 == 0 and k_done:
                            pe.wait_ge(dl_lo, NKEYS * i + k_done)
                        dl_score(i, step, n_done)
                        n_done += 1
                    else:
                        dl_turn(i, step, k_done, n_done)
                        if before is not None:
                            dl_values(i, before, k_done - 1)
                        before = step
                        k_done += 1
                    project(ph, share(units, s, NDL))
                dl_values(i, before, k_done - 1)
                project(ph, share(units, NDL, NDL))

            with pe.Fori(0, NPAIR - 1) as i:
                stick_breaking(i, 2 * i + 1)
                dilated(i, 2 * i + 2, UNITS)
            stick_breaking(NPAIR - 1, 2 * NPAIR - 1)
            dilated(NPAIR - 1, 2 * NPAIR, UNITS_LAST)
            for j in range(2):
                small_group(2 * NPAIR + 1, "M", j)

            def output_part(b, part):
                for n in range(8 * part, 8 * part + 8):
                    half, e, p = n // 24, n % 24 // 3, n % 3
                    y, w = ((y_hi, wo_hi), (y_hi, wo_lo), (y_lo, wo_hi))[p]
                    last = mm(sc_bank[:, 2 * b + half, :], y[:, b, e, :], w[:, e, 512 * half:512 * half + 512],
                              start=(e == 0 and p == 0), stop=(e == 7 and p == 2))
                if part == 5:
                    last.then_inc(out_done, 1)

            def sample(i, br):
                j = 2 * i + br
                kc, vc = kcs[br], vcs[br]
                pe.wait_ge(kv_in[br], KV_LOADS[br] * 16 * (i + 1))
                pe.wait_ge(s_over, j + 1)
                for g in range(4):
                    if g >= 2:
                        pe.wait_ge(kct_set, 4 * j + g - 1)
                    for n in range(4 * g, 4 * g + 4):
                        last = mm(proj_bank[:, g % 2, (n % 4) * P:(n % 4) * P + P], kc[:, n, :], ident, start=True, stop=True,
                                  is_transpose=True)
                    last.then_inc(kct_turned, 1)
                pe.wait_ge(yl_set, j + 1)
                pe.wait_ge(out_norm, j + 1)
                output_part(br, 0)
                pe.wait_ge(kct_set, 4 * j + 4)
                pe.wait_ge(qbd_set, j + 1)
                past = proj_bank[:, 0, 0:256].rearrange("p (g h b q) -> p g h b q", g=2, h=2, b=DB)
                for n in range(16):
                    mm(past[:, n % 2, :, n // 2, :], kct[:, n, :], q_bd[:, :, (n // 2) * DS:(n // 2) * DS + DS],
                       start=True, stop=True)
                mm(proj_bank[0:NSAMP, 0, 256:384], k_s[:], q_bd[:].rearrange("p h n -> p (h n)"), start=True, stop=True)\
                    .then_inc(s_pe, 1)
                output_part(br, 1)
                if br == 0:
                    pe.wait_ge(s_dve, 9 * j + 3)
                    o = proj_bank[:, 1, 0:384].rearrange("p (x n) -> p x n", x=3)
                    mm(o[:, 2, :], tri_f, es[:, 2, :], start=True, stop=True)
                    mm(o[:, 1, :], tri_f, es[:, 1, :], start=True, stop=False)
                    mm(o[:, 1, :], ones_f[:], es[:, 2, :], start=False, stop=True)
                    mm(o[:, 0, :], tri_f, es[:, 0, :], start=True, stop=False)
                    mm(o[:, 0, :], ones_f[:], es[:, 1, :], start=False, stop=False)
                    mm(o[:, 0, :], ones_f[:], es[:, 2, :], start=False, stop=True).then_inc(s_pe, 1)
                    output_part(br, 2)
                    output_part(br, 3)
                else:
                    pe.wait_ge(s_dve, 9 * j + 1)
                    for x in range(3):
                        last = mm(proj_bank[:, 1, x * P:x * P + P], zs[:, x, :], ident, start=True, stop=True, is_transpose=True)
                    last.then_inc(s_pe, 1)
                    output_part(br, 2)
                    pe.wait_ge(s_dve, 9 * j + 4)
                    for x in range(3):
                        last = mm(proj_bank[:, 0, x * P:x * P + P], es[:, x, :], ident, start=True, stop=True, is_transpose=True)
                    last.then_inc(s_pe, 1)
                    output_part(br, 3)
                if br == 0:
                    pe.wait_ge(s_act, 8 * j + 3)
                else:
                    pe.wait_ge(s_act, 8 * j + 2)
                o = o_bank[:, 0, 0:P].rearrange("p (h n) -> p h n", h=2)
                mm(o_bank[:, 0, 0:P], v_new[:, br, :], us[0:NSAMP, 2, :], start=True, stop=False, skip_group_check=True)
                for n in range(16):
                    b = n // 2
                    w = us[:, n % 2, :].rearrange("p (h n) -> p h n", h=2)[:, :, b * DS:b * DS + DS]
                    last = mm(o[:, :, b * DS:b * DS + DS], vc[:, n, :], w, start=False, stop=(n == 15), skip_group_check=True)
                last.then_inc(s_pe, 1 if br else 2)
                output_part(br, 4)
                pe.wait_ge(s_dve, 9 * j + 6)
                mm(o_bank[:, 1, 0:NSAMP], head_mean, t_s[:, 0, :], start=True, stop=True).then_inc(s_pe, 1)
                output_part(br, 5)

            pe.sem_inc(out_done, 1)
            pe.wait_ge(wo_set, 8)
            with pe.Fori(0, NPAIR - 1) as i:
                sample(i, 0)
                sample(i, 1)
            sample(NPAIR - 1, 0)
            sample(NPAIR - 1, 1)
            pe.wait_ge(yl_set, 9)
            pe.wait_ge(out_norm, 9)
            for part in range(6):
                output_part(0, part)

        @block.scalar
        def _(act):
            av = nc.scalar.activation
            act.add_instruction(mybir.InstLoadActFuncSet(name=nc.get_next_instruction_name(), act_func_set_id=EXP_LN_SET,
                                                         engine=mybir.EngineType.Activation, ins=[], outs=[]))

            def evacuate(ph, br, i, groups):
                for kind, j in groups:
                    c0, n_p, n_all = CHUNKS[j]
                    if kind in ("V", "TK"):
                        continue
                    if kind == "M":
                        act.wait_ge(small_free, small_no(ph, (kind, j)) + 1)
                        av(fold_t[:], fold_t[:], ACT.Ln, bias=eps_c[:, 0:1]).then_inc(rooted, 1)
                        act.wait_ge(rooted, 4 * (ph - 1) + 2 * j + 1)
                        av(fold_t[:], fold_t[:], ACT.Exp, scale=-0.5).then_inc(rooted, 1)
                        continue
                    if kind in TILE:
                        act.wait_ge(big_done, big_no(ph, (kind, j)) + 1)
                        src = proj_bank[:, BIG.index((kind, j)) % 2, :]
                    if kind == "K":
                        av(k_hi[:, br, c0:c0 + n_p], src[:, 0:n_p], ACT.Copy).then_inc(hi_set, 1)
                    elif kind == "Q":
                        av(q_hi[:, br, c0:c0 + n_p], src[:, 0:n_p], ACT.Copy,
                           scale=(SCALE if br == 0 else -SCALE)).then_inc(hi_set, 1)
                    elif kind == "G":
                        n = 3 * ph + j
                        act.wait_ge(gate_dve, 3 * n + 1)
                        av(turn[:, j % 2, 0:n_p], turn[:, j % 2, 0:n_p], ACT.Exp).then_inc(gate_act, 1)
                        act.wait_ge(gate_act, 3 * n + 1)
                        av(turn[:, j % 2, 0:n_p], turn[:, j % 2, 0:n_p], ACT.Ln, bias=one_c[:, 0:1]).then_inc(gate_act, 1)
                    else:
                        act.wait_ge(small_done, small_no(ph, (kind, j)) + 1)
                        src = sc_bank[:, 3, :]
                        m = 3 + j
                        before = {3: 16, 4: 48, 5: 32}[m]
                        act.wait_ge(stage_out[m % 2], 64 * ph + before)
                        nb = n_p // P
                        ins = av(stage[:, m % 2, 0:nb, :].rearrange("p b c -> p (b c)"), src[:, 0:n_p], ACT.Copy)
                        if j == 2:
                            ins = av(stage[0:NSAMP, m % 2, 2, :], src[0:NSAMP, 2 * P:3 * P], ACT.Copy)
                        ins.then_inc(stage_v, 1)
                        b0 = c0 // P
                        av(v_st[:, br, b0:b0 + nb, 0:4:3, :], src[:, 0:n_p].rearrange("p (b h d) -> p b h d", b=nb, h=2),
                           ACT.Copy).then_inc(hi_set, 1)

            def follow(ph, groups):
                for kind, j in groups:
                    if kind == "G":
                        n, n_p = 3 * ph + j, CHUNKS[j][1]
                        act.wait_ge(gate_dve, 3 * n + 2)
                        av(turn[:, j % 2, 0:n_p], turn[:, j % 2, 0:n_p], ACT.Exp, scale=-1.0).then_inc(gate_act, 1)

            def fold(n, bank, h, sem_pv, value, gates):
                own, other = slice(HD * h, HD * h + HD), slice(HD * (1 - h), HD * (1 - h) + HD)
                act.wait_ge(sem_pv, value)
                act.wait_ge(folded, n + 1)
                act.wait_ge(gated_set, gates)
                av(fold_t[own, :], o_bank[other, bank, :], ACT.Copy).then_inc(fold_hi, 1)

            def load_table(head):
                act.dma_start(table, c_prompt_table[bass.ds(head, 1)].rearrange("a p n -> (a p) n")).then_inc(table_in, 16)

            def token_stats(t):
                rows, c = (P if t < 8 else NSAMP), 12 + 4 * (t % 2)
                act.wait_ge(x_loaded[t], 16)
                if t >= 2:
                    act.wait_ge(x_scaled, t - 1)
                if t >= 1:
                    act.wait_ge(x_sum, 3 * t)
                av(junk[0:rows, :], x_in[t][0:rows], ACT.Square, accum_out=small[0:rows, c:c + 1]).then_inc(x_sum, 1)
                act.wait_ge(x_sum, 3 * t + 1)
                av(small[0:rows, c + 1:c + 2], small[0:rows, c:c + 1], ACT.Ln, scale=1.0 / D,
                   bias=eps_c[0:rows, 0:1]).then_inc(x_sum, 1)
                act.wait_ge(x_sum, 3 * t + 2)
                av(small[0:rows, c + 2:c + 3], small[0:rows, c + 1:c + 2], ACT.Exp, scale=-0.5).then_inc(x_sum, 1)

            act.wait_ge(consts_set, 1)
            token_stats(0)
            token_stats(1)
            for t in range(9):
                rows = P if t < 8 else NSAMP
                if t + 2 < 9:
                    token_stats(t + 2)
                for half in range(2):
                    n = 2 * t + half
                    act.wait_ge(x_turned, n + 1)
                    av(h_hi[:, 4 * half:4 * half + 4, t * P:t * P + rows],
                       sc_bank[:, n % 3, :].rearrange("p (b n) -> p b n", b=4)[:, :, 0:rows], ACT.Copy).then_inc(hh_set, 1)
                if t in (5, 8):
                    evacuate(0, 0, 0, [("K", t // 3 - 1)])
            load_table(0)
            for s in range(2, len(FIRST) + 1):
                follow(0, FIRST[s - 1])
                if s < len(FIRST):
                    evacuate(0, 0, 0, FIRST[s])

            def beside(ph, br, i, units, s, steps):
                follow(ph, ended(units, s - 1, steps))
                evacuate(ph, br, i, ended(units, s, steps))

            def stick_breaking(i, ph):
                b0 = NSB * i
                beside(ph, 1, i, UNITS, -1, NSB)
                act.wait_ge(folded, 8 * i + 1)

                def width(s):
                    c, kb, h = SB_STEPS[s]
                    return 512 * (c + 1) - max(512 * c, P * kb)

                def exp_z(s):
                    act.wait_ge(sb_cap, b0 + s + 1)
                    av(soft[:, s % 3, 0:width(s)], soft[:, s % 3, 0:width(s)], ACT.Exp).then_inc(sb_exp, 1)

                def ln(s):
                    act.wait_ge(sb_exp, b0 + s + 1)
                    av(soft[:, s % 3, 0:width(s)], soft[:, s % 3, 0:width(s)], ACT.Ln, bias=one_c[:, 0:1]).then_inc(sb_ln, 1)

                def s_high(s):
                    act.wait_ge(sb_soft, b0 + s + 1)
                    if s >= 2:
                        act.wait_ge(sb_sum, b0 + s - 1)
                        carries = sum(kb > 0 for _, kb, _ in SB_STEPS[:s - 1])
                        if SB_STEPS[s - 2][1] > 0:
                            act.wait_ge(sb_comp, SB_CARRIES * i + carries)
                    av(s_hi[:, s % 2, 0:width(s)], soft[:, s % 3, 0:width(s)], ACT.Copy).then_inc(sb_shi, 1)

                exp_z(0)
                ln(0)
                exp_z(1)
                s_high(0)
                ln(1)
                for s in range(NSB):
                    w = width(s)
                    if s + 1 < NSB:
                        s_high(s + 1)
                    act.wait_ge(sb_u, b0 + s + 1)
                    av(z[:, s % 3, 0:w], z[:, s % 3, 0:w], ACT.Exp).then_inc(sb_a, 1)
                    if s + 2 < NSB:
                        exp_z(s + 2)
                    act.wait_ge(sb_a, b0 + s + 1)
                    if s >= 2:
                        act.wait_ge(sb_pv, b0 + s - 1)
                    av(a_hi[:, s % 2, 0:w], z[:, s % 3, 0:w], ACT.Copy).then_inc(sb_ahi, 1)
                    if s + 2 < NSB:
                        ln(s + 2)
                    beside(ph, 1, i, UNITS, s, NSB)
                    if s >= 1 and SB_STEPS[s - 1][1] == 0:
                        c, _, h = SB_STEPS[s - 1]
                        fold(8 * i + 2 * c + h, h, h, sb_pv, b0 + s, 2 * ph)
                fold(8 * i + 3, 1, 1, sb_pv, b0 + NSB, 2 * ph)
                for s in range(NSB, NSB + 2):
                    beside(ph, 1, i, UNITS, s, NSB)

            def dilated(i, ph, units):
                beside(ph, 0, i + 1, units, -1, NDL)
                act.wait_ge(folded, 8 * i + 5)
                n_done = k_done = 0
                for s, (kind, h, g, x) in enumerate(DL_STEPS):
                    if kind == "score":
                        q, length = x % 4, P * (x + 1)
                        act.wait_ge(dl_min, NSCORE * i + n_done + 1)
                        row = prob[:, P_OFF[q]:P_OFF[q] + length]
                        av(row, row, ACT.Exp, scale=-1.0, bias=small[:, 4 + q:5 + q],
                           accum_out=small[:, 8 + q:9 + q]).then_inc(dl_exp, 1)
                        n_done += 1
                        if n_done == 8:
                            load_table(2 * i + 1)
                        elif n_done == 16 and units is UNITS:
                            load_table(2 * i + 2)
                    else:
                        o0 = P * (max(x, 4 * g) - 4 * g)
                        act.wait_ge(dl_turned, NKEYS * i + k_done + 1)
                        if k_done >= 2:
                            act.wait_ge(dl_pv, NKEYS * i + k_done - 1)
                        av(pt_hi[:, x % 2, o0:512], sc_bank[:, TURN_BANK[x % 2], o0:512], ACT.Copy).then_inc(dl_hi, 1)
                        k_done += 1
                    beside(ph, 0, i + 1, units, s, NDL)
                    if kind == "score" and x % 4 == 0 and n_done > 1:
                        pg, h_of = 1 - g, (h if g == 1 else h - 1)
                        fold(8 * i + 4 + 2 * h_of + pg, pg, h_of, dl_pv, NKEYS * i + k_done, 2 * ph)
                fold(8 * i + 7, 1, 1, dl_pv, NKEYS * i + NKEYS, 2 * ph)
                for s in range(NDL, NDL + 2):
                    beside(ph, 0, i + 1, units, s, NDL)

            with act.Fori(0, NPAIR - 1) as i:
                stick_breaking(i, 2 * i + 1)
                dilated(i, 2 * i + 2, UNITS)
            stick_breaking(NPAIR - 1, 2 * NPAIR - 1)
            dilated(NPAIR - 1, 2 * NPAIR, UNITS_LAST)
            evacuate(2 * NPAIR + 1, 0, 0, [("M", 0), ("M", 1)])

            def high(t, b, src=None):
                if not (isinstance(t, int) and t < 2):
                    act.wait_ge(out_done, t)
                    hold(act, "act")
                av(y_hi[:, b], gated[:, :, bass.ds(t * P, P)] if src is None else src, ACT.Copy).then_inc(yh_set, 1)

            def output_norm(t, b):
                act.wait_ge(out_done, t + 2)
                act.wait_ge(y_out[b], (t - b) * 8 + 16)
                c = 12 + 4 * b
                bank = sc_bank[:, 2 * b:2 * b + 2, :].rearrange("p a n -> p (a n)")
                av(m_out[:, b], bank, ACT.Square, accum_out=small[:, c:c + 1]).then_inc(out_root, 1)
                act.wait_ge(out_root, 3 * t + 1)
                av(small[:, c + 1:c + 2], small[:, c:c + 1], ACT.Ln, scale=1.0 / D, bias=eps_c[:, 0:1]).then_inc(out_root, 1)
                act.wait_ge(out_root, 3 * t + 2)
                av(small[:, c + 2:c + 3], small[:, c + 1:c + 2], ACT.Exp, scale=-0.5).then_inc(out_root, 1)

            def sample(i, br, last=False):
                j = 2 * i + br
                for g in range(4):
                    act.wait_ge(kct_turned, 4 * j + g + 1)
                    av(kct[:, 4 * g:4 * g + 4, :].rearrange("p n c -> p (n c)"), proj_bank[:, g % 2, :], ACT.Copy).then_inc(kct_set, 1)
                if not last:
                    high(j + 1, 1 - br)
                if br == 0:
                    act.wait_ge(s_dve, 9 * j + 1)
                    av(es[:], es[:], ACT.Exp).then_inc(s_act, 1)
                    act.wait_ge(s_act, 8 * j + 1)
                    av(es[:], es[:], ACT.Ln, bias=one_c[:, 0:1]).then_inc(s_act, 1)
                    act.wait_ge(s_dve, 9 * j + 4)
                    av(us[:], us[:], ACT.Exp).then_inc(s_act, 1)
                else:
                    act.wait_ge(s_dve, 9 * j + 2)
                    av(es[:].rearrange("p x n -> p (x n)"), proj_bank[:, 1, 0:384], ACT.Exp, scale=-1.0,
                       bias=small[:, 4:5], accum_out=small[:, 8:9]).then_inc(s_act, 1)
                    act.wait_ge(s_pe, 5 * j + 3)
                    av(us[:].rearrange("p x n -> p (x n)"), proj_bank[:, 0, 0:384], ACT.Copy).then_inc(s_act, 2)
                act.wait_ge(s_dve, 9 * j + 6)
                av(g_s[:], g_s[:], ACT.Exp).then_inc(s_act, 1)
                act.wait_ge(s_act, 8 * j + 4)
                av(g_s[:], g_s[:], ACT.Ln, bias=one_c[:, 0:1]).then_inc(s_act, 1)
                act.wait_ge(s_dve, 9 * j + 7)
                av(g_s[:], g_s[:], ACT.Exp, scale=-1.0).then_inc(s_act, 1)
                act.wait_ge(s_pe, 5 * j + 5)
                av(t_s[:, 1, :], o_bank[:, 1, 0:NSAMP], ACT.Ln, bias=eps_c[:, 0:1]).then_inc(s_act, 1)
                act.wait_ge(s_act, 8 * j + 7)
                av(t_s[:, 1, :], t_s[:, 1, :], ACT.Exp, scale=-0.5).then_inc(s_act, 1)
                output_norm(j, br)

            act.wait_ge(gated_set, 18)
            high(0, 0)
            with act.Fori(0, NPAIR - 1) as i:
                sample(i, 0)
                sample(i, 1)
            sample(NPAIR - 1, 0)
            sample(NPAIR - 1, 1, last=True)
            act.wait_ge(s_over, 9)
            high(8, 0, gated_s[:])
            output_norm(8, 0)

        @block.vector
        def _(dve):
            ve = nc.vector

            def last_of(ph):
                return isinstance(ph, int) and ph == 2 * NPAIR - 1

            def evacuate(ph, br, i, groups):
                hi_of = {g: m for m, g in enumerate(
                    [g for g in finished(UNITS_FIRST) if g[0] in ("K", "Q", "TV")])}

                def kept(x):
                    return samp[:, mix(br, i), x, :].rearrange("p a n -> p (a n)")

                for kind, j in groups:
                    c0, n_p, n_all = CHUNKS[j]
                    if kind == "M":
                        n = small_no(ph, (kind, j))
                        dve.wait_ge(small_done, n + 1)
                        ve.tensor_copy(fold_t[:], sc_bank[:, 3, :]).then_inc(small_free, 1)
                        continue
                    if kind in TILE:
                        src, free = proj_bank[:, BIG.index((kind, j)) % 2, :], big_free
                        tail = src[:, n_p:n_all]
                        dve.wait_ge(big_done, big_no(ph, (kind, j)) + 1)
                    else:
                        src, free = sc_bank[:, 3, :], small_free
                        dve.wait_ge(small_done, small_no(ph, (kind, j)) + 1)
                    if (kind, j) in hi_of:
                        dve.wait_ge(hi_set, len(hi_of) * ph + hi_of[(kind, j)] + 1)
                    if kind == "K":
                        ins = ve.tensor_tensor(k_lo[:, br, c0:c0 + n_p], src[:, 0:n_p], k_hi[:, br, c0:c0 + n_p].bitcast(F32),
                                               ALU.subtract)
                        if j == 2:
                            ve.tensor_copy(kept(1), tail)
                            ins = ve.tensor_copy(turn[:, j % 2, n_p:n_all], tail)
                    elif kind == "Q":
                        c = SCALE if br == 0 else -SCALE
                        ins = ve.scalar_tensor_tensor(q_lo[:, br, c0:c0 + n_p], src[:, 0:n_p], c,
                                                      q_hi[:, br, c0:c0 + n_p].bitcast(F32), ALU.mult, ALU.subtract)
                        if j == 2:
                            ins = ve.tensor_scalar(kept(0), tail, c, None, ALU.mult)
                    elif kind == "V":
                        ins = ve.tensor_copy(turn[:, (3 + j) % 2, 0:n_all], src[:, 0:n_all])
                    elif kind == "G":
                        t = gated[:, mix(br, i), c0:c0 + n_p].rearrange("p a n -> p (a n)")
                        ve.tensor_scalar(turn[:, j % 2, 0:n_p], src[:, 0:n_p], -1.0, LINEAR, ALU.mult, ALU.min).then_inc(gate_dve, 1)
                        ins = ve.tensor_copy(t, src[:, 0:n_p])
                        if j == 2:
                            ins = ve.tensor_copy(kept(2), tail)
                    elif kind == "TK":
                        before = {0: 0, 1: 0, 2: 16}[j]
                        if not (isinstance(ph, int) and ph == 0 and before == 0):
                            dve.wait_ge(stage_out[j % 2], 64 * ph + before)
                        nb = n_p // P
                        ins = ve.tensor_copy(stage[:, j % 2, 0:nb, :].rearrange("p b c -> p (b c)"), src[:, 0:n_p])
                        if j == 2:
                            ins = ve.tensor_copy(stage[0:NSAMP, j % 2, 2, :], src[0:NSAMP, 2 * P:3 * P])
                    else:
                        nb, b0 = n_p // P, c0 // P
                        ins = ve.tensor_tensor(v_st[:, br, b0:b0 + nb, 1:3, :],
                                               src[:, 0:n_p].rearrange("p (b h d) -> p b h d", b=nb, h=2),
                                               v_st[:, br, b0:b0 + nb, 0:4:3, :].bitcast(F32), ALU.subtract)
                    ins.then_inc(free, 1)

            def follow(ph, br, i, groups, nxt=True):
                for kind, j in groups:
                    c0, n_p, _ = CHUNKS[j]
                    if kind == "M":
                        gate_chunk(ph, j)
                    elif kind == "G":
                        n = 3 * ph + j
                        g = gated[:, mix(br, i), c0:c0 + n_p].rearrange("p a n -> p (a n)")
                        t = turn[:, j % 2, 0:n_p]
                        dve.wait_ge(gate_act, 3 * n + 2)
                        dve.wait_ge(big_free, big_no(ph, (kind, j)) + 1)
                        ve.scalar_tensor_tensor(t, g, -1.0, t, ALU.mult, ALU.max).then_inc(gate_dve, 1)
                    if kind in TILE and j == 2:
                        if TILE[kind] < 2:
                            split_high(ph, TILE[kind] + 2)
                        elif nxt:
                            split_high(ph + 1, TILE[kind] - 2)

            def finish(ph, br, i, groups):
                for kind, j in groups:
                    if kind == "G":
                        c0, n_p, _ = CHUNKS[j]
                        n = 3 * ph + j
                        g = gated[:, mix(br, i), c0:c0 + n_p].rearrange("p a n -> p (a n)")
                        dve.wait_ge(gate_act, 3 * n + 3)
                        ve.tensor_tensor(g, g, turn[:, j % 2, 0:n_p], ALU.mult).then_inc(gate_dve, 1)

            def beside(ph, br, i, units, s, steps, nxt=True):
                finish(ph, br, i, ended(units, s - 2, steps))
                follow(ph, br, i, ended(units, s - 1, steps), nxt)
                evacuate(ph, br, i, ended(units, s, steps))

            def split_high(ph, t):
                n = 4 * ph + t
                if t >= 2:
                    dve.wait_ge(big_done, big_no(ph, (KINDS[t - 2], 2)) + 1)
                elif not (isinstance(ph, int) and ph == 0):
                    dve.wait_ge(big_done, big_no(ph - 1, (KINDS[t + 2], 2)) + 1)
                for h in range(2):
                    dve.wait_ge(w_loaded[h], 16 * n + 16)
                    if not (isinstance(n, int) and n < 2):
                        dve.wait_ge(w_set, 2 * n - 2)
                    ve.tensor_copy(w_hi[:, t % 2, 4 * h:4 * h + 4, :], w_raw[:, h]).then_inc(w_hi_set, 1)

            def gate_chunk(ph, j):
                n = 2 * (ph - 1) + j
                cs = slice(512 * j, 512 * j + 512)
                tile = tile_of[0]
                dve.wait_ge(rooted, 2 * n + 2)
                ve.tensor_tensor(head_t[:, cs], head_t[:, cs], fold_t[:], ALU.mult).then_inc(normed, 1)
                dve.wait_ge(normed, n + 1)
                y = gated[:, tile, cs].rearrange("p a n -> p (a n)")
                ve.scalar_tensor_tensor(y, head_t[:, cs], norm_w[:, tile], y, ALU.mult, ALU.mult).then_inc(gated_set, 1)

            tile_of = [None]

            def fold(n, bank, h, c):
                own = slice(HD * h, HD * h + HD)
                dve.wait_ge(fold_hi, n + 1)
                ve.tensor_tensor(head_t[own, c * 512:c * 512 + 512], o_bank[own, bank, :], fold_t[own, :], ALU.add)\
                    .then_inc(folded, 1)

            ve.memset(one_c[:], 1.0)
            ve.memset(eps_c[:], EPS).then_inc(consts_set, 1)
            dve.wait_ge(rows_in, 16 * 2)
            ve.tensor_copy(tri[:], consts[:, 2:4, :]).then_inc(consts_set, 1)
            split_high(0, 0)

            def scale_tokens(t):
                rows, c = (P if t < 8 else NSAMP), 12 + 4 * (t % 2)
                dve.wait_ge(x_sum, 3 * t + 3)
                ve.scalar_tensor_tensor(x_in[t][0:rows], x_in[t][0:rows], small[0:rows, c + 2:c + 3], pre_row[0:rows, :],
                                        ALU.mult, ALU.mult).then_inc(x_scaled, 1)

            scale_tokens(0)
            for t in range(9):
                rows = P if t < 8 else NSAMP
                if t + 1 < 9:
                    scale_tokens(t + 1)
                for half in range(2):
                    n = 2 * t + half
                    dve.wait_ge(hh_set, n + 1)
                    dst = (slice(None), slice(4 * half, 4 * half + 4), slice(t * P, t * P + rows))
                    ve.tensor_tensor(h_lo[dst], sc_bank[:, n % 3, :].rearrange("p (b n) -> p b n", b=4)[:, :, 0:rows],
                                     h_hi[dst].bitcast(F32), ALU.subtract).then_inc(hl_set, 1)
                if t == 4:
                    split_high(0, 1)
                if t in (5, 8):
                    evacuate(0, 0, 0, [("K", t // 3 - 1)])
            for s in range(2, len(FIRST) + 2):
                finish(0, 0, 0, FIRST[s - 2])
                if s <= len(FIRST):
                    follow(0, 0, 0, FIRST[s - 1])
                if s < len(FIRST):
                    evacuate(0, 0, 0, FIRST[s])
            dve.wait_ge(consts_in, 16 * 4)
            ve.memset(head_t[:], 0.0)
            ve.memset(gated[:, 3, :], 0.0).then_inc(folded, 1)

            def stick_breaking(i, ph):
                b0 = NSB * i
                tile_of[0] = mix(0, i + 3)
                beside(ph, 1, i, UNITS, -1, NSB, not last_of(ph))
                ve.tensor_copy(small[:, 20:22], bias_all[:, bass.ds(i * 2, 2)]).then_inc(bias_set, 1)
                dve.wait_ge(bias_set, i + 1)

                def shape(s):
                    c, kb, h = SB_STEPS[s]
                    o0 = max(0, P * kb - 512 * c)
                    return c, kb, h, o0, 512 - o0

                def shift(s):
                    c, kb, h, o0, w = shape(s)
                    b = small[:, 20 + h:21 + h]
                    dve.wait_ge(sb_scores, b0 + s + 1)
                    zz, src = z[:, s % 3, :], sc_bank[:, 0, :]
                    if s >= 3:
                        dve.wait_ge(sb_alo, b0 + s - 2)
                    if kb >= 4 * c:
                        ins = ve.scalar_tensor_tensor(zz[:, 0:P], src[:, 0:P], b, diag_mask[:], ALU.add, ALU.add)
                        if w > P:
                            ins = ve.tensor_scalar(zz[:, P:w], src[:, P:w], b, None, ALU.add)
                    else:
                        ins = ve.tensor_scalar(zz[:, 0:w], src[:, 0:w], b, None, ALU.add)
                    ins.then_inc(sb_z, 1)
                    dve.wait_ge(sb_z, b0 + s + 1)
                    if s >= 3:
                        dve.wait_ge(sb_slo, b0 + s - 2)
                    ve.tensor_scalar(soft[:, s % 3, 0:w], zz[:, 0:w], LINEAR, None, ALU.min).then_inc(sb_cap, 1)

                def softplus(s):
                    w = shape(s)[4]
                    dve.wait_ge(sb_ln, b0 + s + 1)
                    ve.tensor_tensor(soft[:, s % 3, 0:w], soft[:, s % 3, 0:w], z[:, s % 3, 0:w], ALU.max).then_inc(sb_soft, 1)

                shift(0)
                shift(1)
                softplus(0)
                softplus(1)
                for s in range(NSB):
                    c, kb, h, o0, w = shape(s)
                    dve.wait_ge(sb_sum, b0 + s + 1)
                    dve.wait_ge(sb_soft, b0 + s + 1)
                    ve.tensor_tensor(z[:, s % 3, 0:w], z[:, s % 3, 0:w], sc_bank[:, 1 + h, o0:512], ALU.subtract).then_inc(sb_u, 1)
                    if s + 2 < NSB:
                        shift(s + 2)
                    dve.wait_ge(sb_ahi, b0 + s + 1)
                    if s >= 2:
                        dve.wait_ge(sb_pv, b0 + s - 1)
                    ve.tensor_tensor(a_lo[:, s % 2, 0:w], z[:, s % 3, 0:w], a_hi[:, s % 2, 0:w].bitcast(F32), ALU.subtract)\
                        .then_inc(sb_alo, 1)
                    if s + 2 < NSB:
                        softplus(s + 2)
                    beside(ph, 1, i, UNITS, s, NSB, not last_of(ph))
                    if s >= 1 and SB_STEPS[s - 1][1] == 0:
                        cc, _, hh = SB_STEPS[s - 1]
                        fold(8 * i + 2 * cc + hh, hh, hh, cc)
                fold(8 * i + 3, 1, 1, 1)
                for s in range(NSB, NSB + 3):
                    beside(ph, 1, i, UNITS, s, NSB, not last_of(ph))

            def dilated(i, ph, units):
                tile_of[0] = mix(0, i)
                beside(ph, 0, i + 1, units, -1, NDL)
                n_done = k_done = 0
                for s, (kind, h, g, x) in enumerate(DL_STEPS):
                    if kind == "score":
                        q, length = x % 4, P * (x + 1)
                        dve.wait_ge(dl_scores, NSCORE * i + n_done + 1)
                        if x == 0:
                            dve.wait_ge(table_in, 32 * i + 16 * h + 16)
                        if k_done:
                            dve.wait_ge(dl_turned, NKEYS * i + k_done)
                        bank = sc_bank[:, 0:2, :].rearrange("p a n -> p (a n)")
                        row = prob[:, P_OFF[q]:P_OFF[q] + length]
                        hold(dve, "dve")
                        ve.tensor_tensor_reduce(out=row, in0=bank[:, 0:length], in1=table[:, 1024 - length:1024],
                                                scale=1.0, scalar=3.0 * FAR, op0=ALU.add, op1=ALU.min,
                                                accum_out=small[:, 4 + q:5 + q]).then_inc(dl_min, 1)
                        dve.wait_ge(dl_exp, NSCORE * i + n_done + 1)
                        ve.reciprocal(small[:, 8 + q:9 + q], small[:, 8 + q:9 + q]).then_inc(dl_rec, 1)
                        dve.wait_ge(dl_rec, NSCORE * i + n_done + 1)
                        ve.tensor_scalar(row, row, small[:, 8 + q:9 + q], None, ALU.mult).then_inc(dl_prob, 1)
                        n_done += 1
                    else:
                        o0 = P * (max(x, 4 * g) - 4 * g)
                        dve.wait_ge(dl_hi, NKEYS * i + k_done + 1)
                        ve.tensor_tensor(pt_lo[:, x % 2, o0:512], sc_bank[:, TURN_BANK[x % 2], o0:512],
                                         pt_hi[:, x % 2, o0:512].bitcast(F32), ALU.subtract).then_inc(dl_lo, 1)
                        k_done += 1
                    beside(ph, 0, i + 1, units, s, NDL)
                    if kind == "score" and x % 4 == 0 and n_done > 1:
                        pg, h_of = 1 - g, (h if g == 1 else h - 1)
                        fold(8 * i + 4 + 2 * h_of + pg, pg, h_of, pg)
                fold(8 * i + 7, 1, 1, 1)
                for s in range(NDL, NDL + 3):
                    beside(ph, 0, i + 1, units, s, NDL)

            with dve.Fori(0, NPAIR - 1) as i:
                stick_breaking(i, 2 * i + 1)
                dilated(i, 2 * i + 2, UNITS)
            stick_breaking(NPAIR - 1, 2 * NPAIR - 1)
            dilated(NPAIR - 1, 2 * NPAIR, UNITS_LAST)
            tile_of[0] = slice(7, 8)
            for j in range(2):
                evacuate(2 * NPAIR + 1, 0, 0, [("M", j)])
                gate_chunk(2 * NPAIR + 1, j)

            ve.memset(q_bd[:], 0.0)
            ve.memset(gated_s[:], 0.0)
            ve.memset(ones_f[:], 1.0).then_inc(consts_set, 1)
            dve.wait_ge(consts_set, 3)
            dve.wait_ge(pages_in, 48)
            ve.memset(small[:, 23:24], 0.0).then_inc(out_norm, 2)
            ve.memset(small[:, 22:23], 0.0).then_inc(s_over, 1)

            def output_scale(t, b):
                dve.wait_ge(out_root, 3 * t + 3)
                c = 12 + 4 * b
                bank = sc_bank[:, 2 * b:2 * b + 2, :].rearrange("p a n -> p (a n)")
                ve.scalar_tensor_tensor(m_out[:, b], bank, small[:, c + 2:c + 3], post_row[:], ALU.mult, ALU.mult)\
                    .then_inc(out_norm, 1)

            def sample(i, br):
                j = 2 * i + br
                d = 9 * j
                q = samp[:, mix(br, i), 0, :].rearrange("p a n -> p (a n)")
                gate_in = samp[:, mix(br, i), 2, :].rearrange("p a n -> p (a n)")
                dve.wait_ge(s_over, j + 1)
                ve.tensor_copy(k_s[:], samp[:, mix(br, i), 1, :].rearrange("p a n -> p (a n)"))
                ve.tensor_copy(q_bd[0:HD, 0, :], q[0:HD])
                ve.tensor_copy(q_bd[HD:P, 1, :], q[HD:P]).then_inc(qbd_set, 1)
                past, new = proj_bank[:, 0, 0:256], proj_bank[0:NSAMP, 0, 256:384]
                dve.wait_ge(s_pe, 5 * j + 1)
                if br == 0:
                    ve.memset(zs[HD:P, 2, :], -FAR)
                    ve.tensor_copy(small[:, 20:22], bias_all[:, bass.ds(i * 2, 2)]).then_inc(bias_set, 1)
                    dve.wait_ge(bias_set, NPAIR + 2 * i + 1)
                    for h in range(2):
                        b = small[:, 20 + h:21 + h]
                        hs = slice(h * HD, h * HD + HD)
                        ve.tensor_scalar(zs[:, 0:2, hs], past.rearrange("p (g n) -> p g n", g=2)[:, :, hs], b, None, ALU.add)
                        ins = ve.scalar_tensor_tensor(zs[0:NSAMP, 2, hs], new[:, hs], b[0:NSAMP], s_mask[:], ALU.add, ALU.add)
                    ins.then_inc(bias_set, 1)
                    dve.wait_ge(bias_set, NPAIR + 2 * i + 2)
                    ve.tensor_scalar(es[:], zs[:], LINEAR, None, ALU.min).then_inc(s_dve, 1)
                    dve.wait_ge(s_act, 8 * j + 2)
                    ve.tensor_tensor(es[:], es[:], zs[:], ALU.max).then_inc(s_dve, 2)
                    dve.wait_ge(s_pe, 5 * j + 2)
                    ve.tensor_tensor(us[:].rearrange("p x n -> p (x n)"), zs[:].rearrange("p x n -> p (x n)"),
                                     proj_bank[:, 1, 0:384], ALU.subtract).then_inc(s_dve, 1)
                else:
                    dve.wait_ge(kv_in[1], KV_LOADS[1] * 16 * (i + 1))
                    ve.memset(zs[HD:P, 2, :], FAR)
                    ve.tensor_tensor(zs[:, 0:2, :].rearrange("p x n -> p (x n)"), past,
                                     s_table[:, 0:2, :].rearrange("p x n -> p (x n)"), ALU.add)
                    ve.tensor_tensor(zs[0:NSAMP, 2, :], new, s_table[0:NSAMP, 2, :], ALU.add).then_inc(s_dve, 1)
                    dve.wait_ge(s_pe, 5 * j + 2)
                    ve.tensor_reduce(small[:, 4:5], proj_bank[:, 1, 0:384], AX.X, ALU.min).then_inc(s_dve, 1)
                    dve.wait_ge(s_act, 8 * j + 1)
                    ve.reciprocal(small[:, 8:9], small[:, 8:9]).then_inc(s_dve, 1)
                    dve.wait_ge(s_dve, d + 3)
                    ve.tensor_scalar(es[:], es[:], small[:, 8:9], None, ALU.mult).then_inc(s_dve, 1)
                dve.wait_ge(s_pe, 5 * j + 4)
                ve.tensor_copy(o_s[0:HD], o_bank[0:HD, 0, 0:HD])
                ve.tensor_copy(o_s[HD:P], o_bank[HD:P, 0, HD:P]).then_inc(s_dve, 1)
                dve.wait_ge(s_dve, d + 5)
                ve.tensor_tensor(t_s[:, 0, :], o_s[:], o_s[:], ALU.mult)
                ve.tensor_scalar(g_s[:], gate_in, -1.0, LINEAR, ALU.mult, ALU.min).then_inc(s_dve, 1)
                dve.wait_ge(s_act, 8 * j + 5)
                ve.scalar_tensor_tensor(g_s[:], gate_in, -1.0, g_s[:], ALU.mult, ALU.max).then_inc(s_dve, 1)
                dve.wait_ge(s_act, 8 * j + 6)
                ve.tensor_tensor(g_s[:], g_s[:], gate_in, ALU.mult).then_inc(s_dve, 1)
                dve.wait_ge(s_act, 8 * j + 8)
                ve.tensor_tensor(o_s[:], o_s[:], t_s[:, 1, :], ALU.mult).then_inc(s_dve, 1)
                dve.wait_ge(s_dve, d + 9)
                out = gated_s[:, mix(br, i), 0:NSAMP].rearrange("p a n -> p (a n)")
                ve.scalar_tensor_tensor(out, o_s[:], norm_w[:, mix(br, i)], g_s[:], ALU.mult, ALU.mult).then_inc(s_over, 1)
                output_scale(j, br)

            with dve.Fori(0, NPAIR - 1) as i:
                sample(i, 0)
                sample(i, 1)
            sample(NPAIR - 1, 0)
            sample(NPAIR - 1, 1)
            output_scale(8, 0)

        @block.gpsimd
        def _(pool):
            gp = nc.gpsimd

            def split_low(ph, kind, h, nxt=True):
                n = 4 * ph + TILE[kind] + 2
                if TILE[kind] >= 2 and not nxt:
                    return
                pool.wait_ge(w_hi_set, 2 * n + h + 1)
                ks = slice(4 * h, 4 * h + 4)
                t = TILE[kind] % 2
                gp.tensor_tensor(w_lo[:, t, ks, :], w_raw[:, h], w_hi[:, t, ks, :].bitcast(F32), ALU.subtract)\
                    .then_inc(w_set, 1)

            def beside(ph, br, units, s, steps, nxt=True):
                for kind, j in ended(units, s - 2, steps):
                    if kind in TILE and j == 2:
                        split_low(ph, kind, 1, nxt)
                for kind, j in ended(units, s - 1, steps):
                    if kind in TILE and j == 2:
                        split_low(ph, kind, 0, nxt)
                    if (kind, j) == ("M", 0):
                        square_chunk(ph, 1)
                for group in ended(units, s, steps):
                    if group[0] == "K":
                        join_k(ph, br, group[1])

            def join_k(ph, br, j):
                c0, n_p, _ = CHUNKS[j]
                pool.wait_ge(big_free, big_no(ph, ("K", j)) + 1)
                if not (isinstance(ph, int) and ph == 0):
                    pool.wait_ge(gate_dve, 9 * ph)
                gp.tensor_tensor(turn[:, j % 2, 0:n_p], k_hi[:, br, c0:c0 + n_p].bitcast(F32),
                                 k_lo[:, br, c0:c0 + n_p].bitcast(F32), ALU.add).then_inc(turn_set, 1)

            def square_chunk(ph, j):
                if j == 0:
                    pool.wait_ge(folded, 4 * (ph - 1) + 1)
                else:
                    pool.wait_ge(gated_set, 2 * (ph - 1) + 1)
                cs = slice(512 * j, 512 * j + 512)
                gp.tensor_tensor(fold_t[:], head_t[:, cs], head_t[:, cs], ALU.mult).then_inc(squared, 1)

            for kind in ("Q", "G"):
                for h in range(2):
                    split_low(-1, kind, h)
            for (kind, j), in FIRST:
                if kind == "K":
                    join_k(0, 0, j)
                if kind in TILE and j == 2:
                    split_low(0, kind, 0)
                    split_low(0, kind, 1)

            def stick_breaking(i, ph, nxt=True):
                b0 = NSB * i
                square_chunk(ph, 0)
                beside(ph, 1, UNITS, -1, NSB, nxt)

                def s_low(s):
                    c, kb, h = SB_STEPS[s]
                    w = 512 * (c + 1) - max(512 * c, P * kb)
                    pool.wait_ge(sb_shi, b0 + s + 1)
                    gp.tensor_tensor(s_lo[:, s % 2, 0:w], soft[:, s % 3, 0:w], s_hi[:, s % 2, 0:w].bitcast(F32), ALU.subtract)\
                        .then_inc(sb_slo, 1)

                s_low(0)
                for s in range(NSB):
                    if s + 1 < NSB:
                        s_low(s + 1)
                    beside(ph, 1, UNITS, s, NSB, nxt)
                for s in range(NSB, NSB + 3):
                    beside(ph, 1, UNITS, s, NSB, nxt)

            def dilated(i, ph, units):
                square_chunk(ph, 0)
                for s in range(-1, NDL + 3):
                    beside(ph, 0, units, s, NDL)

            with pool.Fori(0, NPAIR - 1) as i:
                stick_breaking(i, 2 * i + 1)
                dilated(i, 2 * i + 2, UNITS)
            stick_breaking(NPAIR - 1, 2 * NPAIR - 1, False)
            dilated(NPAIR - 1, 2 * NPAIR, UNITS_LAST)
            for e in range(8):
                pool.wait_ge(wo_in[e % 2], 16 * (e // 2 + 1))
                gp.tensor_copy(wo_hi[:, e, :], wo_raw[:, e % 2]).then_inc(wo_hi_set, 1)
                pool.wait_ge(wo_hi_set, e + 1)
                gp.tensor_tensor(wo_lo[:, e, :], wo_raw[:, e % 2], wo_hi[:, e, :].bitcast(F32), ALU.subtract).then_inc(wo_set, 1)
            square_chunk(2 * NPAIR + 1, 0)
            square_chunk(2 * NPAIR + 1, 1)

            def low(t, b, src=None):
                pool.wait_ge(yh_set, t + 1)
                gp.tensor_tensor(y_lo[:, b], gated[:, :, bass.ds(t * P, P)] if src is None else src,
                                 y_hi[:, b].bitcast(F32), ALU.subtract).then_inc(yl_set, 1)

            def residual(t, b, rows=P):
                pool.wait_ge(out_norm, t + 3)
                pool.wait_ge(x2_in[b], 8 * (t - b) + 16)
                gp.tensor_tensor(m_out[0:rows, b], m_out[0:rows, b], x_out[0:rows, b], ALU.add).then_inc(out_sum, 1)

            low(0, 0)
            with pool.Fori(0, NPAIR - 1) as i:
                low(2 * i + 1, 1)
                residual(2 * i, 0)
                low(2 * i + 2, 0)
                residual(2 * i + 1, 1)
            low(7, 1)
            residual(6, 0)
            residual(7, 1)
            low(8, 0, gated_s[:])
            residual(8, 0, NSAMP)


def _constants():
    import numpy as np
    k = np.arange(128)
    sq = np.zeros((128, 6, 128), np.float32)
    sq[:, 0] = np.eye(128)
    sq[:, 1] = (k[:, None] // 64 == k[None, :] // 64) / 64.0
    sq[:, 2] = k[:, None] >= k[None, :]
    sq[:, 3] = k[:, None] < k[None, :]
    sq[:, 4] = 1.0
    sq[:, 5] = np.where(k[:, None] < k[None, :], 0.0, -1e30)

    def term(dist, slope):
        n = sum((dist >= 0) & (dist % r == 0) & (dist <= w) for w, r in ((128, 1), (512, 4), (2048, 16)))
        n = n.astype(np.int64)
        return np.where(n > 0, slope * dist - np.log(np.maximum(n, 1)), 1e30).astype(np.float32)

    slopes = 2.0 ** (-np.arange(1, 9, dtype=np.float64))
    x = np.arange(1024)
    prompt = np.stack([term(k[:, None] + 896 - x[None, :], s) for s in slopes])
    sample = np.full((4, 128, 3, 2, 8, 8), 1e30, np.float32)
    q = np.arange(8)
    for p in range(4):
        for h in range(2):
            s = slopes[2 * p + h]
            for g in range(2):
                sample[p, :, g, h] = term(256 + q[None, :] - (128 * g + k[:, None]), s)[:, None, :]
            for b in range(8):
                sample[p, 8 * b:8 * b + 8, 2, h, b] = term(q[None, :] - q[:, None], s)
    mask = np.full((64, 8, 8), -1e30, np.float32)
    for b in range(8):
        mask[8 * b:8 * b + 8, b] = np.where(q[:, None] < q[None, :], 0.0, -1e30)
    return {"c_square": sq, "c_prompt_table": prompt, "c_sample_table": sample.reshape(4, 128, 3, 128),
            "c_sample_mask": mask.reshape(64, 64)}


_INS = ["x_prompt", "x_sample", "cache_k_sb", "cache_v_sb", "cache_k_dil", "cache_v_dil", "page_table", "pre_norm_w",
        "w_in", "sb_bias", "sb_norm_w", "dil_norm_w", "w_out", "post_norm_w"]
_OUTS = [(1, 1024, 1024), (8, 8, 1024), (1, 1, 1024, 8, 64), (1, 1, 1024, 8, 64), (1, 8, 8, 8, 64), (1, 8, 8, 8, 64),
         (1, 1, 1024, 8, 64), (1, 1, 1024, 8, 64), (1, 8, 264, 8, 64), (1, 8, 264, 8, 64)]


def kernel(**inputs):
    import numpy as _np
    import concourse.bacc as _bacc
    from concourse import mybir as _mybir
    from concourse.bass_utils import run_bass_kernel_spmd as _run

    nc = _bacc.Bacc("TRN2", target_bir_lowering=False, num_devices=1, dynamic_dma_scratch_size=1024)
    arrays, args = {}, []
    given = {n: _np.ascontiguousarray(inputs[n]) for n in _INS}
    given.update(_constants())
    for name, a in given.items():
        arrays[f"in_{name}_dram"] = a
        args.append(nc.dram_tensor(f"in_{name}_dram", a.shape, _mybir.dt.from_np(a.dtype), kind="ExternalInput").ap())
    for i, shape in enumerate(_OUTS):
        args.append(nc.dram_tensor(f"out_{i}_dram", shape, _mybir.dt.float32, kind="ExternalOutput").ap())
    hymba_step(nc, *args)
    r = _run(nc, [arrays], core_ids=[0])
    return tuple(r.results[0][f"out_{i}_dram"] for i in range(len(_OUTS)))
```
